# Optimizing a Trainium2 kernel written in Bass

```python
import math
import jax, jax.numpy as jnp
from jax import lax
import numpy as np

D_MODEL = 1024
BATCH = 1
SEQ = 512
DEPTH = 2

N_EVEN = (DEPTH + 1) // 2
N_ODD = DEPTH // 2

HG_HEADS = 4
HG_DK = 128
HG_DV = 128
HG_WIDTH = HG_HEADS * HG_DK
HG_CHUNK = 32

CV_CH = D_MODEL - HG_HEADS * HG_DV
CV_K = 31

IN_COLS = 4 * HG_WIDTH + 2 * CV_CH

POOL_WINDOWS = (2, 4, 8, 16)
POOL_GROUPS = len(POOL_WINDOWS)
POOL_CH = D_MODEL // POOL_GROUPS

MEM_LEN = 256
XA_HEADS = 4
XA_DH = D_MODEL // XA_HEADS

D_FF = -(-(8 * D_MODEL) // (3 * 256)) * 256

ALPHA = (2 * DEPTH) ** 0.25
BETA = (8 * DEPTH) ** -0.25
LN_EPS = 1e-5
RMS_EPS = 1e-6


def layer_norm(x, g, b):
    xf = x.astype(jnp.float32)
    mu = jnp.mean(xf, axis=-1, keepdims=True)
    var = jnp.mean(jnp.square(xf - mu), axis=-1, keepdims=True)
    y = (xf - mu) * lax.rsqrt(var + LN_EPS) * g.astype(jnp.float32) + b.astype(jnp.float32)
    return y.astype(x.dtype)

def hgrn2_chunked(q, k, v, log_f):
    B, S, H, DK = q.shape
    DV = v.shape[-1]
    nc = S // HG_CHUNK

    def to_chunks(t):
        return t.astype(jnp.float32).reshape(B, nc, HG_CHUNK, H, t.shape[-1]).transpose(0, 3, 1, 2, 4)

    q, k, v, log_f = to_chunks(q), to_chunks(k), to_chunks(v), to_chunks(log_f)
    b = jnp.cumsum(log_f, axis=3)
    b_last = b[:, :, :, -1:, :]
    q_t = q * jnp.exp(b)
    k_t = k * jnp.exp(-b)
    causal = jnp.tril(jnp.ones((HG_CHUNK, HG_CHUNK), dtype=bool))
    scores = jnp.einsum('bhntd,bhnsd->bhnts', q_t, k_t)
    scores = jnp.where(causal, scores, 0.0)
    o_intra = jnp.einsum('bhnts,bhnsv->bhntv', scores, v)
    k_end = k * jnp.exp(b_last - b)
    d_state = jnp.einsum('bhnsd,bhnsv->bhndv', k_end, v)
    decay = jnp.exp(b_last[:, :, :, 0, :])

    def step(state, inp):
        dec, ds = inp
        return dec[..., None] * state + ds, state

    s0 = jnp.zeros((B, H, DK, DV), jnp.float32)
    _, s_start = lax.scan(step, s0, (jnp.moveaxis(decay, 2, 0), jnp.moveaxis(d_state, 2, 0)))
    s_start = jnp.moveaxis(s_start, 0, 2)
    o_inter = jnp.einsum('bhntd,bhndv->bhntv', q_t, s_start)
    o = o_intra + o_inter
    return o.transpose(0, 2, 3, 1, 4).reshape(B, S, H, DV)

def hybrid_ab_mixer(x, w_in, lb, hg_norm_g, cv_w, cv_b, cv_ln_g, cv_ln_b, w_out):
    B, S, _ = x.shape
    h = x @ w_in
    q, f_pre, i_v, g, a, a_gate = jnp.split(
        h, [HG_WIDTH, 2 * HG_WIDTH, 3 * HG_WIDTH, 4 * HG_WIDTH, 4 * HG_WIDTH + CV_CH], axis=-1)

    lb = lb.astype(jnp.float32)
    f_pre = f_pre.astype(jnp.float32)
    f = lb + (1.0 - lb) * jax.nn.sigmoid(f_pre)
    k = (1.0 - lb) * jax.nn.sigmoid(-f_pre)
    log_f = jnp.log(f)
    heads = lambda t: t.reshape(B, S, HG_HEADS, -1)
    o = hgrn2_chunked(heads(q), heads(k), heads(i_v), heads(log_f))
    o = o * lax.rsqrt(jnp.mean(jnp.square(o), axis=-1, keepdims=True) + RMS_EPS)
    o = o.reshape(B, S, HG_HEADS * HG_DV) * hg_norm_g.astype(jnp.float32) * jax.nn.silu(g.astype(jnp.float32))

    u = a * jax.nn.sigmoid(a_gate)
    u = lax.conv_general_dilated(
        u, cv_w.astype(u.dtype), window_strides=(1,), padding=[(CV_K - 1, 0)],
        dimension_numbers=('NWC', 'WIO', 'NWC'), feature_group_count=CV_CH) + cv_b
    u = jax.nn.silu(layer_norm(u, cv_ln_g, cv_ln_b))

    y = jnp.concatenate([o.astype(x.dtype), u.astype(x.dtype)], axis=-1)
    return y @ w_out

def multiscale_pool_mixer(x, pool_w, pool_scale):
    B, S, _ = x.shape
    xg = x.astype(jnp.float32).reshape(B, S, POOL_GROUPS, POOL_CH)
    cs = jnp.cumsum(xg, axis=1)
    pos = jnp.arange(1, S + 1, dtype=jnp.float32)
    feats = []
    for gi, w in enumerate(POOL_WINDOWS):
        c = cs[:, :, gi]
        lagged = jnp.pad(c, ((0, 0), (w, 0), (0, 0)))[:, :S]
        mean = (c - lagged) / jnp.minimum(pos, float(w))[:, None]
        feats.append(mean - xg[:, :, gi])
    p = jnp.stack(feats, axis=2).astype(x.dtype)
    y = jnp.einsum('bsgc,gcd->bsgd', p, pool_w).reshape(B, S, D_MODEL)
    return y * pool_scale

def memory_cross_attention(x, mem_n, w_q, w_k, w_v, w_o):
    B, S, _ = x.shape
    q = (x @ w_q).reshape(B, S, XA_HEADS, XA_DH)
    k = (mem_n @ w_k).reshape(B, -1, XA_HEADS, XA_DH)
    v = (mem_n @ w_v).reshape(B, -1, XA_HEADS, XA_DH)
    s = jnp.einsum('bshd,bmhd->bhsm', q, k).astype(jnp.float32) * (XA_DH ** -0.5)
    p = jax.nn.softmax(s, axis=-1).astype(x.dtype)
    o = jnp.einsum('bhsm,bmhd->bshd', p, v).reshape(B, S, D_MODEL)
    return o @ w_o

def swiglu_ffn(x, w_gate, w_up, w_down):
    return (jax.nn.silu(x @ w_gate) * (x @ w_up)) @ w_down

def first_inputs(seed: int = 0) -> dict:
    key = jax.random.key(seed)
    ks = jax.random.split(key, 32)
    f32 = jnp.float32
    nrm = lambda k, shape, scale: jax.random.normal(k, shape, f32) * scale
    gain = lambda k, shape: 1.0 + 0.02 * jax.random.normal(k, shape, f32)
    bias = lambda k, shape: 0.02 * jax.random.normal(k, shape, f32)
    d = D_MODEL
    return {
        "x": jax.random.normal(ks[0], (BATCH, SEQ, d), f32),
        "mem": jax.random.normal(ks[1], (BATCH, MEM_LEN, d), f32),
        "lb_param": nrm(ks[2], (DEPTH + 1, HG_WIDTH), 0.1),
        "mem_ln_g": gain(ks[3], (d,)),
        "mem_ln_b": bias(ks[4], (d,)),
        "ab_w_in": nrm(ks[5], (N_EVEN, d, IN_COLS), d ** -0.5),
        "hg_norm_g": gain(ks[6], (N_EVEN, HG_HEADS * HG_DV)),
        "cv_w": nrm(ks[7], (N_EVEN, CV_K, 1, CV_CH), CV_K ** -0.5),
        "cv_b": bias(ks[8], (N_EVEN, CV_CH)),
        "cv_ln_g": gain(ks[9], (N_EVEN, CV_CH)),
        "cv_ln_b": bias(ks[10], (N_EVEN, CV_CH)),
        "ab_w_out": nrm(ks[11], (N_EVEN, d, d), BETA * d ** -0.5),
        "pool_w": nrm(ks[12], (N_ODD, POOL_GROUPS, POOL_CH, POOL_CH), BETA * POOL_CH ** -0.5),
        "pool_scale": gain(ks[13], (N_ODD, d)),
        "ln_mix_g": gain(ks[14], (DEPTH, d)),
        "ln_mix_b": bias(ks[15], (DEPTH, d)),
        "xa_wq": nrm(ks[16], (DEPTH, d, d), d ** -0.5),
        "xa_wk": nrm(ks[17], (DEPTH, d, d), d ** -0.5),
        "xa_wv": nrm(ks[18], (DEPTH, d, d), d ** -0.5),
        "xa_wo": nrm(ks[19], (DEPTH, d, d), BETA * d ** -0.5),
        "ln_xa_g": gain(ks[20], (DEPTH, d)),
        "ln_xa_b": bias(ks[21], (DEPTH, d)),
        "ffn_wg": nrm(ks[22], (DEPTH, d, D_FF), d ** -0.5),
        "ffn_wu": nrm(ks[23], (DEPTH, d, D_FF), d ** -0.5),
        "ffn_wd": nrm(ks[24], (DEPTH, D_FF, d), BETA * D_FF ** -0.5),
        "ln_ffn_g": gain(ks[25], (DEPTH, d)),
        "ln_ffn_b": bias(ks[26], (DEPTH, d)),
    }

def first_block(x, mem, lb_param, mem_ln_g, mem_ln_b, ab_w_in, hg_norm_g, cv_w, cv_b,
              cv_ln_g, cv_ln_b, ab_w_out, pool_w, pool_scale, ln_mix_g, ln_mix_b,
              xa_wq, xa_wk, xa_wv, xa_wo, ln_xa_g, ln_xa_b, ffn_wg, ffn_wu, ffn_wd,
              ln_ffn_g, ln_ffn_b):
    lb_all = jnp.cumsum(jax.nn.softmax(lb_param.astype(jnp.float32), axis=0), axis=0)
    mem_n = layer_norm(mem, mem_ln_g, mem_ln_b)
    for l in range(DEPTH):
        if l % 2 == 0:
            e = l // 2
            y = hybrid_ab_mixer(x, ab_w_in[e], lb_all[l], hg_norm_g[e], cv_w[e], cv_b[e],
                                cv_ln_g[e], cv_ln_b[e], ab_w_out[e])
        else:
            o = l // 2
            y = multiscale_pool_mixer(x, pool_w[o], pool_scale[o])
        x = layer_norm(ALPHA * x + y, ln_mix_g[l], ln_mix_b[l])
        y = memory_cross_attention(x, mem_n, xa_wq[l], xa_wk[l], xa_wv[l], xa_wo[l])
        x = layer_norm(ALPHA * x + y, ln_xa_g[l], ln_xa_b[l])
        y = swiglu_ffn(x, ffn_wg[l], ffn_wu[l], ffn_wd[l])
        x = layer_norm(ALPHA * x + y, ln_ffn_g[l], ln_ffn_b[l])
    return x


N_A_LAYERS = DEPTH // 2
N_B_LAYERS = DEPTH - N_A_LAYERS

GLA_HEADS = 4
GLA_KEY_DIM = D_MODEL // 2
GLA_VAL_DIM = D_MODEL
GLA_HK = GLA_KEY_DIM // GLA_HEADS
GLA_HV = GLA_VAL_DIM // GLA_HEADS
GLA_GATE_RANK = 16
GLA_GATE_NORM = 16.0
GLA_CHUNK = 64
A_PROJ = 2 * GLA_KEY_DIM + 2 * GLA_VAL_DIM + GLA_GATE_RANK

SWA_HEAD_DIM = 64
SWA_Q_HEADS = D_MODEL // SWA_HEAD_DIM
SWA_GROUP = 8
SWA_KV_HEADS = SWA_Q_HEADS // SWA_GROUP
WINDOW = 128
BLOCK = 128
KV_PROJ = 2 * SWA_KV_HEADS * SWA_HEAD_DIM

REL_BUCKETS = 32
REL_MAX_DIST = 128

D_FF_2 = 4 * D_MODEL
EPS = 1e-6
NEG = -1e30


def rmsnorm(x, g):
    xf = x.astype(jnp.float32)
    y = xf * lax.rsqrt(jnp.mean(xf * xf, axis=-1, keepdims=True) + EPS) * g.astype(jnp.float32)
    return y.astype(x.dtype)

def sq_relu_mlp(h, w_up, w_down):
    u = jax.nn.relu(h @ w_up)
    return (u * u) @ w_down

def gla_mixer(h, w_in, w_gk2, b_gk, g_onorm, w_out):
    B, T, _ = h.shape
    C = GLA_CHUNK
    NC = T // C
    f32 = jnp.float32
    proj = h @ w_in
    q, k, v, gate, glr = jnp.split(
        proj, [GLA_KEY_DIM, 2 * GLA_KEY_DIM, 2 * GLA_KEY_DIM + GLA_VAL_DIM,
               2 * GLA_KEY_DIM + 2 * GLA_VAL_DIM], axis=-1)
    gk = jax.nn.log_sigmoid((glr @ w_gk2 + b_gk).astype(f32)) / GLA_GATE_NORM

    def heads(t, d):
        return t.astype(f32).reshape(B, NC, C, GLA_HEADS, d).transpose(1, 0, 3, 2, 4)

    qf = heads(q, GLA_HK) * (GLA_HK ** -0.5)
    kf = heads(k, GLA_HK)
    vf = heads(v, GLA_HV)
    bcum = jnp.cumsum(heads(gk, GLA_HK), axis=-2)
    q_t = qf * jnp.exp(bcum)
    k_t = kf * jnp.exp(-bcum)
    causal = jnp.asarray(np.tril(np.ones((C, C), dtype=bool)))
    attn = jnp.where(causal, jnp.einsum('nbhik,nbhjk->nbhij', q_t, k_t), 0.0)
    o_intra = jnp.einsum('nbhij,nbhjv->nbhiv', attn, vf)
    b_last = bcum[..., -1:, :]
    k_dec = kf * jnp.exp(b_last - bcum)

    def step(S, xs):
        q_c, k_c, v_c, bl = xs
        o = jnp.einsum('bhik,bhkv->bhiv', q_c, S)
        S = S * jnp.exp(bl)[..., 0, :, None] + jnp.einsum('bhjk,bhjv->bhkv', k_c, v_c)
        return S, o

    S0 = jnp.zeros((B, GLA_HEADS, GLA_HK, GLA_HV), f32)
    _, o_inter = lax.scan(step, S0, (q_t, k_dec, vf, b_last))
    o = (o_intra + o_inter).transpose(1, 0, 3, 2, 4).reshape(B, T, GLA_HEADS, GLA_HV)
    o = o * lax.rsqrt(jnp.mean(o * o, axis=-1, keepdims=True) + EPS) * g_onorm.astype(f32)
    o = o * jax.nn.silu(gate.astype(f32).reshape(B, T, GLA_HEADS, GLA_HV))
    return o.reshape(B, T, GLA_VAL_DIM).astype(h.dtype) @ w_out

def rel_bucket_band():
    i = np.arange(BLOCK)[:, None]
    j = np.arange(2 * BLOCK)[None, :]
    dist = i + BLOCK - j
    n = np.maximum(dist, 0)
    max_exact = REL_BUCKETS // 2
    large = max_exact + (np.log(np.maximum(n, 1) / max_exact)
                         / np.log(REL_MAX_DIST / max_exact)
                         * (REL_BUCKETS - max_exact)).astype(np.int32)
    large = np.minimum(large, REL_BUCKETS - 1)
    bucket = np.where(n < max_exact, n, large).astype(np.int32)
    valid = (dist >= 0) & (dist < WINDOW)
    return bucket, valid

def shared_kv(h, w_kv):
    B, T, _ = h.shape
    NB = T // BLOCK
    k, v = jnp.split(h @ w_kv, 2, axis=-1)

    def band(t):
        t = t.reshape(B, NB, BLOCK, SWA_KV_HEADS, SWA_HEAD_DIM)
        prev = jnp.concatenate([jnp.zeros_like(t[:, :1]), t[:, :-1]], axis=1)
        return jnp.concatenate([prev, t], axis=2)

    return band(k), band(v)

def swa_mixer(h, kb, vb, w_q, sinks, rel_table, w_out):
    B, T, _ = h.shape
    NB = T // BLOCK
    q = (h @ w_q).reshape(B, NB, BLOCK, SWA_KV_HEADS, SWA_GROUP, SWA_HEAD_DIM)
    s = jnp.einsum('bnqhgd,bnkhd->bnhgqk', q, kb).astype(jnp.float32) * (SWA_HEAD_DIM ** -0.5)
    bucket, valid = rel_bucket_band()
    bias = rel_table.astype(jnp.float32)[bucket]
    bias = bias.transpose(2, 0, 1).reshape(SWA_KV_HEADS, SWA_GROUP, BLOCK, 2 * BLOCK)
    first = (np.arange(NB)[:, None] == 0) & (np.arange(2 * BLOCK)[None, :] < BLOCK)
    mask = jnp.asarray(valid[None] & ~first[:, None, :])
    s = jnp.where(mask[None, :, None, None], s + bias, NEG)
    sink = sinks.astype(jnp.float32).reshape(SWA_KV_HEADS, SWA_GROUP, 1, 1)
    m = jnp.maximum(jnp.max(s, axis=-1, keepdims=True), sink)
    p = jnp.exp(s - m)
    p = p / (jnp.sum(p, axis=-1, keepdims=True) + jnp.exp(sink - m))
    o = jnp.einsum('bnhgqk,bnkhd->bnqhgd', p.astype(vb.dtype), vb)
    return o.reshape(B, T, SWA_Q_HEADS * SWA_HEAD_DIM) @ w_out

def second_inputs(seed: int = 0) -> dict:
    key = jax.random.key(seed)
    ks = jax.random.split(key, 20)
    f32 = jnp.float32

    def w(k, shape, fan_in, scale=1.0):
        return jax.random.normal(k, shape, f32) * (scale * fan_in ** -0.5)

    def gain(k, shape):
        return 1.0 + 0.02 * jax.random.normal(k, shape, f32)

    return {
        "x": jax.random.normal(ks[0], (BATCH, SEQ, D_MODEL), f32),
        "a_w_in": w(ks[1], (N_A_LAYERS, D_MODEL, A_PROJ), D_MODEL),
        "a_w_gk2": w(ks[2], (N_A_LAYERS, GLA_GATE_RANK, GLA_KEY_DIM), GLA_GATE_RANK),
        "a_b_gk": 0.1 * jax.random.normal(ks[3], (N_A_LAYERS, GLA_KEY_DIM), f32),
        "a_onorm": gain(ks[4], (N_A_LAYERS, GLA_HV)),
        "a_w_out": w(ks[5], (N_A_LAYERS, GLA_VAL_DIM, D_MODEL), GLA_VAL_DIM),
        "kv_norm": gain(ks[6], (D_MODEL,)),
        "w_kv": w(ks[7], (D_MODEL, KV_PROJ), D_MODEL),
        "b_w_q": w(ks[8], (N_B_LAYERS, D_MODEL, SWA_Q_HEADS * SWA_HEAD_DIM), D_MODEL),
        "b_sinks": 0.5 * jax.random.normal(ks[9], (N_B_LAYERS, SWA_Q_HEADS), f32),
        "b_w_out": w(ks[10], (N_B_LAYERS, SWA_Q_HEADS * SWA_HEAD_DIM, D_MODEL), D_MODEL),
        "rel_table": 0.5 * jax.random.normal(ks[11], (REL_BUCKETS, SWA_Q_HEADS), f32),
        "ln_mix": gain(ks[12], (DEPTH, D_MODEL)),
        "ln_mlp": gain(ks[13], (DEPTH, D_MODEL)),
        "w_up": w(ks[14], (DEPTH, D_MODEL, D_FF_2), D_MODEL),
        "w_down": w(ks[15], (DEPTH, D_FF_2, D_MODEL), D_FF_2, scale=0.5),
        "ln_final": gain(ks[16], (D_MODEL,)),
    }

def second_block(x, a_w_in, a_w_gk2, a_b_gk, a_onorm, a_w_out, kv_norm, w_kv, b_w_q, b_sinks,
              b_w_out, rel_table, ln_mix, ln_mlp, w_up, w_down, ln_final):
    h = x
    kb = vb = None
    for layer in range(DEPTH):
        if layer < N_A_LAYERS:
            h = h + gla_mixer(rmsnorm(h, ln_mix[layer]), a_w_in[layer], a_w_gk2[layer],
                              a_b_gk[layer], a_onorm[layer], a_w_out[layer])
        else:
            if layer == N_A_LAYERS:
                kb, vb = shared_kv(rmsnorm(h, kv_norm), w_kv)
            j = layer - N_A_LAYERS
            h = h + swa_mixer(rmsnorm(h, ln_mix[layer]), kb, vb, b_w_q[j], b_sinks[j],
                              rel_table, b_w_out[j])
        h = h + sq_relu_mlp(rmsnorm(h, ln_mlp[layer]), w_up[layer], w_down[layer])
    return rmsnorm(h, ln_final)


def setup_inputs(seed=0):
    out = dict(first_inputs(seed))
    for name, value in second_inputs(seed + 1).items():
        if name != "x":
            out[name + "_2"] = value
    return out


def reference(
    x, mem, lb_param, mem_ln_g, mem_ln_b, ab_w_in, hg_norm_g, cv_w, cv_b, cv_ln_g, cv_ln_b,
    ab_w_out, pool_w, pool_scale, ln_mix_g, ln_mix_b, xa_wq, xa_wk, xa_wv, xa_wo, ln_xa_g,
    ln_xa_b, ffn_wg, ffn_wu, ffn_wd, ln_ffn_g, ln_ffn_b, a_w_in_2, a_w_gk2_2, a_b_gk_2,
    a_onorm_2, a_w_out_2, kv_norm_2, w_kv_2, b_w_q_2, b_sinks_2, b_w_out_2, rel_table_2,
    ln_mix_2, ln_mlp_2, w_up_2, w_down_2, ln_final_2,
):
    x = first_block(
        x, mem, lb_param, mem_ln_g, mem_ln_b, ab_w_in, hg_norm_g, cv_w, cv_b, cv_ln_g, cv_ln_b,
        ab_w_out, pool_w, pool_scale, ln_mix_g, ln_mix_b, xa_wq, xa_wk, xa_wv, xa_wo, ln_xa_g,
        ln_xa_b, ffn_wg, ffn_wu, ffn_wd, ln_ffn_g, ln_ffn_b,
    )
    return second_block(
        x, a_w_in_2, a_w_gk2_2, a_b_gk_2, a_onorm_2, a_w_out_2, kv_norm_2, w_kv_2, b_w_q_2,
        b_sinks_2, b_w_out_2, rel_table_2, ln_mix_2, ln_mlp_2, w_up_2, w_down_2, ln_final_2,
    )


_drawn_inputs = setup_inputs


def setup_inputs(seed=0):
    import zlib

    import numpy as np

    out = dict(_drawn_inputs(seed))
    spreads = {}
    factors = {'lb_param': 4.502,
     'mem_ln_g': 8.0,
     'mem_ln_b': 3.469,
     'hg_norm_g': 8.0,
     'cv_b': 5.804,
     'cv_ln_g': 8.0,
     'cv_ln_b': 8.0,
     'pool_scale': 6.3,
     'a_onorm_2': 4.872,
     'kv_norm_2': 8.0,
     'b_sinks_2': 35.172,
     'ln_mlp_2': 3.784,
     'ln_final_2': 7.449}
    for name, (base, spread) in spreads.items():
        noise = np.random.default_rng([zlib.crc32(name.encode()), seed]).standard_normal(out[name].shape)
        drawn = base * np.exp(spread * noise) if base else spread * noise
        out[name] = __import__('jax').numpy.asarray(drawn.astype(out[name].dtype))
    for name, factor in factors.items():
        out[name] = (out[name] * factor).astype(out[name].dtype)
    return out
```

```python
import math
from contextlib import ExitStack

import numpy as np

import concourse.bass as bass
from concourse import mybir

F32 = mybir.dt.float32
F32R = mybir.dt.float32r
U32 = mybir.dt.uint32
ACT = mybir.ActivationFunctionType
ALU = mybir.AluOpType
AX = mybir.AxisListType

D, T, P = 1024, 512, 128
KT = D // P
TT = T // P
MEM = 256
MT = MEM // P
UNIT = 2048
FFN_CHUNKS = 2816 // 256
MLP_CHUNKS = 4096 // 256
TAPS = 31
HEADS = 4
ALPHA = 4.0 ** 0.25
LN_EPS, RMS_EPS = 1e-5, 1e-6
NEG = -1e30
POOL_W = (2, 4, 8, 16)

STAGES = [("ag0", 1), ("a0", 1), ("ag1", 1), ("f", 2), ("g", 2), ("a1", 1), ("q", 2), ("v", 2),
          ("mk0", 4), ("mv0", 4), ("mixo", 4), ("mk1a", 2), ("xq0", 4), ("xo0", 4), ("mk1b", 2),
          ("ffn0", 3 * FFN_CHUNKS), ("mv1a", 2), ("pool", 1), ("mv1b", 2), ("xq1", 4), ("xo1", 4),
          ("ffn1", 3 * FFN_CHUNKS), ("glr", 1), ("gq", 2), ("gk", 2), ("gg", 4), ("gv", 4), ("go", 4),
          ("mlp0", 2 * MLP_CHUNKS), ("sk", 1), ("sv", 1), ("sq", 4), ("so", 4), ("mlp1", 2 * MLP_CHUNKS)]
UNITS = {}
N_UNITS = 0
for _name, _n in STAGES:
    UNITS[_name] = N_UNITS
    N_UNITS += _n

PARAMS = [("mem_g", 8), ("mem_b", 8), ("lb", 12), ("hg_g", 4), ("cv_b", 4), ("cv_g", 4), ("cv_lb", 4),
          ("cv_w", 4 * TAPS), ("pool_s", 8),
          ("mix_g0", 8), ("mix_b0", 8), ("mix_g1", 8), ("mix_b1", 8),
          ("xa_g0", 8), ("xa_b0", 8), ("xa_g1", 8), ("xa_b1", 8),
          ("ffn_g0", 8), ("ffn_b0", 8), ("ffn_g1", 8), ("ffn_b1", 8),
          ("b_gk", 4), ("onorm", 2), ("kvn", 8), ("mix2_g0", 8), ("mix2_g1", 8), ("mlp2_g0", 8),
          ("mlp2_g1", 8), ("fin_g", 8)]
COL = {}
N_PARAMS = 0
for _name, _n in PARAMS:
    COL[_name] = N_PARAMS
    N_PARAMS += _n

CONSTS = [("ident", 128), ("flip", 128), ("mask32", 128), ("mask64", 128), ("scan32", 512), ("scan64", 512),
          ("invpos", 16), ("onehot", 384)]
CCOL = {}
N_CONSTS = 0
for _name, _n in CONSTS:
    CCOL[_name] = N_CONSTS
    N_CONSTS += _n


def rel_buckets():
    n = np.arange(128)
    large = 16 + (np.log(np.maximum(n, 1) / 16) / np.log(128 / 16) * 16).astype(np.int32)
    return np.where(n < 16, n, np.minimum(large, 31)).astype(np.int32)


def constants():
    c = np.zeros((128, N_CONSTS), np.float32)

    def put(name, a):
        c[:a.shape[0], CCOL[name]:CCOL[name] + a.shape[1]] = a

    i, j = np.arange(128)[:, None], np.arange(128)[None, :]
    put("ident", (i == j).astype(np.float32))
    put("flip", (i + j == 127).astype(np.float32))
    put("mask32", ((i <= j) & (i // 32 == j // 32)).astype(np.float32))
    put("mask64", ((i <= j) & (i // 64 == j // 64)).astype(np.float32))
    t = np.arange(512)
    put("scan32", np.broadcast_to((t % 32 != 0).astype(np.float32), (128, 512)))
    put("scan64", np.broadcast_to((t % 64 != 0).astype(np.float32), (128, 512)))
    put("invpos", np.broadcast_to((1.0 / np.arange(1, 17)).astype(np.float32), (128, 16)))
    hot = np.zeros((33, 384), np.float32)
    bucket = rel_buckets()
    for e in range(384):
        dist = 255 - e
        hot[bucket[dist] if 0 <= dist < 128 else 32, e] = 1.0
    put("onehot", hot)
    return c


FILL = {}


def plan_banks():
    used, full = [0] * 8, [0] * 8

    def fill(key, bank, unit=None):
        FILL[key] = (bank, used[bank], 0, unit, full[bank] + 1, 0)
        used[bank] += 1
        full[bank] += unit is None

    def loop(trips, units_per_trip, fills):
        per = [sum(f[1] == b for f in fills) for b in range(8)]
        per_full = [sum(f[1] == b and f[2] is None for f in fills) for b in range(8)]
        u, v = list(used), list(full)
        for key, b, unit in fills:
            FILL[key] = (b, u[b], per[b], unit, v[b] + 1, per_full[b] if unit is None else units_per_trip)
            u[b] += 1
            v[b] += unit is None
        for b in range(8):
            used[b] += trips * per[b]
            full[b] += trips * per_full[b]

    def pair(stage, j):
        n = UNITS[stage] + j
        fill((stage, j, 0), 2 * (n % 2))
        fill((stage, j, 1), 2 * (n % 2) + 1, n)

    def pairs(stage, n):
        for j in range(n):
            pair(stage, j)

    def norm(name, has_mean=True):
        if has_mean:
            fill((name, "mean"), 6)
        fill((name, "sq"), 7)

    def gla():
        for h in range(HEADS + 1):
            if h < HEADS:
                fill(("gla", "scores", h), 4)
                fill(("gla", "kend", h), 5)
            if h:
                fill(("gla", "ssq", h - 1), 3)
            if h == HEADS:
                break
            fill(("gla", "o", h, 0), 6)
            fill(("gla", "o", h, 1), 7)
            for t in range(TT):
                fill(("gla", "ds", h, t), t)

    def linear_attention(name, filler):
        for h in range(HEADS):
            fill((name, "scores", h), 4)
            fill((name, "kend", h), 5)
            if filler:
                pair(*filler[2 * h])
            if h:
                fill((name, "ssq", h - 1), 6 + h % 2)
            fill((name, "o", h, 0), 6 + h % 2)
            fill((name, "ds", h, 0), 4)
            fill((name, "ds", h, 1), 5)
            if filler:
                pair(*filler[2 * h + 1])
            fill((name, "ds", h, 2), 4)
            fill((name, "ds", h, 3), 5)
        fill((name, "ssq", HEADS - 1), 6)

    def queries_ahead(stage, step, steps):
        for j in range(4):
            if j >= 2:
                step(j - 2)
            pair(stage, j)
        for s in range(2, steps):
            step(s)

    def cross(name):
        def step(h):
            if h < HEADS:
                fill((name, "s", h, 0), 4)
                fill((name, "s", h, 1), 5)
            if h >= 2:
                for d in range(2):
                    fill((name, "o", h - 2, d), 2 * (h % 2) + d)
            if 1 <= h <= HEADS:
                fill((name, "pT", h - 1, 0), 6)
                fill((name, "pT", h - 1, 1), 7)
        return step

    def swa(it):
        if it < SWA_ITEMS:
            for j in range(2):
                fill(("swa", "s", it, j), 4 + 2 * (it % 2) + j)
        if it >= 2 and it % 2 == 0:
            fill(("swa", "o", (it - 2) // 2), 2 + it // 2 % 2)
        if 1 <= it <= SWA_ITEMS:
            for j in range(2):
                fill(("swa", "pT", it - 1, j), j)

    def ups(name, tag, c, gated):
        f = []
        if gated:
            f += [((name, tag, "g", 0), 0, None), ((name, tag, "g", 1), 1, c)]
            c += 1
        b = 2 if gated else 0
        return f + [((name, tag, "u", 0), b, None), ((name, tag, "u", 1), b + 1, c)]

    def downs(name, tag, c):
        return [((name, tag, "d", m), 4 + m % 4, c if m == KT - 1 else None) for m in range(KT)]

    def chunks(name, gated):
        c, k = UNITS[name], 2 if gated else 1
        for f in ups(name, "first", c, gated):
            fill(*f)
        c += k
        trips = LOOP_TRIPS[gated]
        loop(trips, 2 * (k + 1), ups(name, 0, c, gated) + downs(name, 0, c + k)
             + ups(name, 1, c + k + 1, gated) + downs(name, 1, c + 2 * k + 1))
        c += trips * 2 * (k + 1)
        if not gated:
            for f in ups(name, "late", c, gated) + downs(name, "late", c + k):
                fill(*f)
            c += k + 1
        for f in downs(name, "last", c):
            fill(*f)

    pairs("ag0", 1), pairs("a0", 1), pairs("ag1", 1), pairs("f", 2)
    norm("memn")
    pairs("g", 2), pairs("a1", 1), pairs("q", 2), pairs("v", 2)
    linear_attention("hg", HG_FILLER)
    norm("cvn")
    for l in range(2):
        if l == 0:
            pairs("mixo", 4)
        else:
            for m in range(KT):
                fill(("pool", 0, m), (4 + m) % 8, UNITS["pool"] if m == KT - 1 else None)
        norm(f"mixn{l}")
        pairs(FILLER[f"mixn{l}"], 2)
        queries_ahead(f"xq{l}", cross(f"xa{l}"), HEADS + 2)
        pairs(f"xo{l}", 4)
        norm(f"xan{l}")
        if l == 0:
            pairs(FILLER["xan0"], 2)
        chunks(f"ffn{l}", True)
        norm(f"ffnn{l}")
        if l == 0:
            pairs(FILLER["ffnn0"], 2)
    fill(("glr", 0, 0), 2 * (UNITS["glr"] % 2), UNITS["glr"])
    norm("r0", False)
    fill(("r0", "tok"), 6)
    for h in range(HEADS):
        fill(("gkz", h), 4 + h)
    pairs("gq", 2), pairs("gk", 2), pairs("gg", 4), pairs("gv", 4)
    gla()
    pairs("go", 4)
    fill(("vec", 0), 4)
    norm("r1", False)
    chunks("mlp0", False)
    for m in range(2):
        fill(("bias", m), 4 + m % 2)
    norm("r2", False)
    fill(("r2", "tok"), 6)
    pairs("sk", 1)
    for m in range(2, 8):
        fill(("bias", m), 4 + m % 2)
    fill(("sv", 0, 0), 2 * (UNITS["sv"] % 2), UNITS["sv"])
    queries_ahead("sq", swa, SWA_ITEMS + 2)
    pairs("so", 4)
    norm("r3", False)
    chunks("mlp1", False)
    norm("fin", False)


LOOP_TRIPS = {True: (FFN_CHUNKS - 1) // 2, False: (MLP_CHUNKS - 2) // 2}
FILLER = {"mixn0": "mk1a", "xan0": "mk1b", "ffnn0": "mv1a", "mixn1": "mv1b"}
SUMMED = 2
HG_FILLER = [("mk0", j) for j in range(4)] + [("mv0", j) for j in range(4)]
SWA_ITEMS = 16
plan_banks()


def at(i, per, c):
    return c if i is None else i * per + c


class Tally:

    def __init__(self, eng, sem):
        self.eng, self.sem, self.n, self.i, self.per = eng, sem, 0, None, 0

    def step(self, ins):
        ins.then_inc(self.sem, 1)
        self.n += 1
        return self.n

    def wait(self, n=None):
        self.eng.wait_ge(self.sem, at(self.i, self.per, self.n if n is None else n))

    def enter(self, i, per):
        self.i, self.per, self.start = i, per, self.n

    def leave(self, trips):
        assert self.n - self.start == self.per, (self.n - self.start, self.per)
        self.n = self.start + trips * self.per
        self.i = None


class Seen:

    def __init__(self, eng, sems):
        self.eng, self.sems, self.n = eng, sems, {}

    def next(self, name, k=1):
        self.n[name] = self.n.get(name, 0) + k
        self.eng.wait_ge(self.sems[name], self.n[name])

    def skip(self, name, k):
        self.n[name] = self.n.get(name, 0) + k


SIGNALS = [
    "x_hi",
    "tile_ready",
    "sq_ready",
    "sq_used",
    "msq_ready",
    "var_ready",
    "rstd_ready",
    "zn_ready",
    "xn_ready",
    "memsq_ready", "memz_ready", "memn_ready", "mem_ready",
    "lbd_ready", "lbe_ready",
    "f_ready", "logf_ready", "b_ready",
    "eb_ready", "kq_ready",
    "inter_done",
    "osq_ready", "y_ready",
    "conv_ready",
    "rowmax_ready", "p_ready",
    "hh_ready", "h_ready", "hf_ready",
    "pool_ready", "glow_ready", "z_ready", "lsig_ready",
    "tok_ready", "rtok_ready", "sum_ready", "e_ready",
    "gate_ready", "scaled", "kpad_ready",
    "out_ready",
]


def build(nc, x, mem, params, consts, table, w_gk2, sinks, w, out):
    scratch = nc.dram_tensor("rel_scratch", [16, 384], F32, kind="Internal").ap()
    with ExitStack() as ctx:
        def sb(stack, name, shape, dt=F32):
            return stack.enter_context(nc.sbuf_tensor(name, shape, dt))

        def new_sem(name):
            return ctx.enter_context(nc.semaphore(name))

        sem = {n: new_sem(n) for n in SIGNALS}
        raw_loaded = [new_sem(f"raw_loaded{s}") for s in range(2)]
        x_loaded = [new_sem(f"x_loaded{s}") for s in range(4)]
        mem_loaded, prm_loaded, ident_loaded = new_sem("mem_loaded"), new_sem("prm_loaded"), new_sem("ident_loaded")
        scan32_loaded, hmask_loaded = new_sem("scan32_loaded"), new_sem("hmask_loaded")
        invpos_loaded, sinks_loaded, table_loaded = new_sem("invpos_loaded"), new_sem("sinks_loaded"), new_sem("table_loaded")
        wgk_loaded, scan64_loaded, gmask_loaded = new_sem("wgk_loaded"), new_sem("scan64_loaded"), new_sem("gmask_loaded")
        onehot_loaded, vec_stored, hankel_loaded = new_sem("onehot_loaded"), new_sem("vec_stored"), new_sem("hankel_loaded")
        flip_loaded = new_sem("flip_loaded")
        w_hi_ready, w_lo_ready, unit_used = new_sem("w_hi_ready"), new_sem("w_lo_ready"), new_sem("unit_used")
        bank_full = [new_sem(f"bank_full{b}") for b in range(8)]
        bank_free = [new_sem(f"bank_free{b}") for b in range(8)]
        act_steps, dve_steps, out_stored = new_sem("act_steps"), new_sem("dve_steps"), new_sem("out_stored")
        ones_ready = new_sem("ones_ready")

        w_raw = sb(ctx, "w_raw", [P, 2, UNIT])
        w_hi = sb(ctx, "w_hi", [P, 2, UNIT], F32R)
        w_lo = sb(ctx, "w_lo", [P, 2, UNIT], F32R)
        xs = sb(ctx, "xs", [P, KT, T])
        xh = sb(ctx, "xh", [P, KT, T], F32R)
        alias = ExitStack()
        kend_hg = sb(alias, "kend_hg", [P, KT, T])[:, KT // 2:, :]
        alias.close()
        xl = sb(ctx, "xl", [P, KT, T], F32R)
        prm = sb(ctx, "prm", [P, N_PARAMS])
        ident = sb(ctx, "ident", [P, P])
        ones = sb(ctx, "ones", [P, P])
        skb = sb(ctx, "skb", [P, 16])
        tab = sb(ctx, "tab", [33, 16])
        sum_x = sb(ctx, "sum_x", [P, T])
        sum_q = sb(ctx, "sum_q", [P, T])
        sq = sb(ctx, "sq", [P, 2, T])
        mean = sb(ctx, "mean", [P, T])
        rstd = sb(ctx, "rstd", [P, T])
        rtok = sb(ctx, "rtok", [P, TT])
        lbs = sb(ctx, "lbs", [P, 3, 4])
        lbm = sb(ctx, "lbm", [P, 4])
        lb0 = sb(ctx, "lb0", [P, 4])
        lb1 = sb(ctx, "lb1", [P, 4])
        rmax = sb(ctx, "rmax", [P, 2, TT])
        rsum = sb(ctx, "rsum", [P, 2, TT])
        rsnk = sb(ctx, "rsnk", [P, 2, TT])
        rinv = sb(ctx, "rinv", [P, 2, TT])
        hdec = sb(ctx, "hdec", [P, 2, 16])

        first = ExitStack()
        memh = sb(first, "memh", [P, KT, MEM], F32R)
        meml = sb(first, "meml", [P, KT, MEM], F32R)
        mk = sb(first, "mk", [P, KT, MEM])
        mv = sb(first, "mv", [P, MT * D])
        PAD = 16
        invpos = sb(first, "invpos", [P, PAD])
        mixer = ExitStack()
        hb = sb(mixer, "hb", [P, HEADS, T])
        hk = sb(mixer, "hk", [P, HEADS, T])
        hq = sb(mixer, "hq", [P, HEADS, T])
        hv = sb(mixer, "hv", [P, TT, HEADS * P])
        hg = sb(mixer, "hg", [P, HEADS, T])
        cu = sb(mixer, "cu", [P, 2, TAPS - 1 + T])
        cacc = sb(mixer, "cacc", [P, 4, T])
        hs = sb(mixer, "hs", [P, 8 * P])
        heb = sb(mixer, "heb", [P, T])
        henb = sb(mixer, "henb", [P, T])
        hmask = sb(mixer, "hmask", [P, P])
        mixer.close()
        mk1 = sb(first, "mk1", [P, KT, MEM])
        mv1 = sb(first, "mv1", [P, MT * D])
        keys, values = [mk, mk1], [mv, mv1]
        cross_mem = ExitStack()
        qf = sb(cross_mem, "qf", [P, KT, T])
        pr = sb(cross_mem, "pr", [P, 2, TT, MEM])
        pT = sb(cross_mem, "pT", [P, 2, MT, T])
        cross_mem.close()
        ffn_mem = ExitStack()
        sil = sb(ffn_mem, "sil", [P, 2, T])
        fh = sb(ffn_mem, "fh", [P, 2, T])
        fhh = sb(ffn_mem, "fhh", [P, 2, 2, T], F32R)
        fhl = sb(ffn_mem, "fhl", [P, 2, 2, T], F32R)
        ffn_mem.close()
        pool_mem = ExitStack()
        pa = sb(pool_mem, "pa", [P, KT, PAD + T])
        pb = sb(pool_mem, "pb", [P, 2, PAD + T])
        ptmp = sb(pool_mem, "ptmp", [P, 2, PAD])
        pp = sb(pool_mem, "pp", [P, KT, T])
        pool_mem.close()
        first.close()

        second = ExitStack()
        mh = sb(second, "mh", [P, 2, 2, T])
        kend_gla = sb(alias, "kend_gla", [P, TT, 2 * P])[:, :, :]
        alias.close()
        mhh = sb(second, "mhh", [P, 2, 2, T], F32R)
        gs = sb(alias, "gs", [P, 8 * 2 * P])
        alias.close()
        mhl = sb(second, "mhl", [P, 2, 2, T], F32R)
        gla_mem = ExitStack()
        gb = sb(gla_mem, "gb", [P, HEADS, T])
        gk = sb(gla_mem, "gk", [P, HEADS, T])
        gq = sb(gla_mem, "gq", [P, HEADS, T])
        gv = sb(gla_mem, "gv", [P, TT, D])
        geb = sb(gla_mem, "geb", [P, T])
        genb = sb(gla_mem, "genb", [P, T])
        gmask = sb(gla_mem, "gmask", [P, P])
        wgk = sb(gla_mem, "wgk", [P, HEADS * P])
        scan64 = sb(gla_mem, "scan64", [P, T])
        gg = sb(gla_mem, "gg", [P, KT, T])
        gla_mem.close()
        glow = mh[:, 0, 0, :]
        swa_mem = ExitStack()
        sf = sb(swa_mem, "sf", [P, KT * T])
        bias = sb(swa_mem, "bias", [P, 16, 2 * P])
        kk = sb(swa_mem, "kk", [P, 2, T])
        vt = sb(swa_mem, "vt", [P, TT * P])
        flip = sb(swa_mem, "flip", [P, P])
        y_mem = ExitStack()
        yh = sb(y_mem, "yh", [P, KT, T], F32R)
        yl = sb(y_mem, "yl", [P, KT, T], F32R)
        y_mem.close()
        spT = sb(y_mem, "spT", [P, 2, 2, T])
        y_mem.close()
        swa_mem.close()
        second.close()

        banks = [ctx.enter_context(nc.psum_tensor(f"bank{b}", [P, T], F32)) for b in range(8)]

        def bank(key):
            return banks[FILL[key][0]]

        def wait_full(eng, key, i=None):
            b, _, _, unit, n, per = FILL[key]
            if unit is None:
                eng.wait_ge(bank_full[b], at(i, per, n))
            else:
                eng.wait_ge(unit_used, at(i, per, unit + 1))

        def wait_free(eng, key, i=None):
            b, n, per = FILL[key][:3]
            if n:
                eng.wait_ge(bank_free[b], at(i, per, n))

        def wait_drained(eng, key, i=None):
            b, n, per = FILL[key][:3]
            eng.wait_ge(bank_free[b], at(i, per, n + 1))

        def free(ins, key):
            ins.then_inc(bank_free[FILL[key][0]], 1)

        def col(name, k=0):
            c = COL[name] + k
            return prm[:, c:c + 1]

        LN_TAIL = {"mixn0": "mix", "mixn1": "mix", "xan0": "xa", "xan1": "xa", "ffnn0": "ffn", "ffnn1": "ffn"}

        def pair_keys(stage, n=4):
            return [(stage, j, m) for j in range(n) for m in range(2)]

        def last_down_keys(name):
            return [(name, "last", "d", m) for m in range(KT)]

        chunk_base = {"ffn0": 0, "ffn1": FFN_CHUNKS, "mlp0": 2 * FFN_CHUNKS, "mlp1": 2 * FFN_CHUNKS + MLP_CHUNKS}
        gated = {"ffn0": True, "ffn1": True, "mlp0": False, "mlp1": False}

        block = ctx.enter_context(nc.Block())

        @block.sync
        def _(sp):
            def load(s, n):
                sp.dma_start(w_raw[:, s, :], w[n, :, :]).then_inc(raw_loaded[s], 16)

            sp.dma_start(xs[:, 0:2, :], x[:, 0:2, :]).then_inc(x_loaded[0], 16)
            load(0, 0)
            for c in range(1, 4):
                sp.dma_start(xs[:, 2 * c:2 * c + 2, :], x[:, 2 * c:2 * c + 2, :]).then_inc(x_loaded[c], 16)
            load(1, 1)
            with sp.Fori(1, N_UNITS // 2) as i:
                for s in range(2):
                    sp.wait_ge(w_lo_ready, i * 2 + (s - 1))
                    sp.dma_start(w_raw[:, s, :], w[bass.ds(i * 2 + s, 1), :, :].rearrange("a p n -> p (a n)"))\
                      .then_inc(raw_loaded[s], 16)
            for k in range(KT):
                sp.wait_ge(sem["out_ready"], k + 1)
                sp.dma_start(out[:, k, :], xs[:, k, :]).then_inc(out_stored, 16)
            sp.wait_ge(out_stored, 16 * KT)

        @block.gpsimd
        def _(pool):
            def const(dst, name, signal, rows=P):
                c = CCOL[name]
                pool.dma_start(dst, consts[0:rows, c:c + dict(CONSTS)[name]]).then_inc(signal, 16)

            pool.memset(ones[:, :], 1.0).then_inc(ones_ready, 1)
            pool.wait_ge(ones_ready, 1)
            pool.memset(cu[:, :, 0:TAPS - 1], 0.0).then_inc(ones_ready, 1)
            pool.dma_start(prm[:, :], params).then_inc(prm_loaded, 16)
            pool.dma_start(mk[:, :, :], mem).then_inc(mem_loaded, 16)
            const(sum_q[:, :], "scan32", scan32_loaded)
            const(hmask[:, :], "mask32", hmask_loaded)
            const(ident[:, :], "ident", ident_loaded)
            const(invpos[:, :], "invpos", invpos_loaded)
            pool.dma_start(skb[:, :], sinks.partition_broadcast(P)).then_inc(sinks_loaded, 16)
            pool.wait_ge(ones_ready, 2)
            pool.memset(tab[32:33, :], NEG).then_inc(ones_ready, 1)
            pool.dma_start(tab[0:32, :], table[0:32, :]).then_inc(table_loaded, 16)
            pool.wait_ge(unit_used, UNITS["glr"])
            pool.wait_ge(ones_ready, 3)
            pool.memset(wgk[96:128, :], 0.0).then_inc(ones_ready, 1)
            pool.wait_ge(ones_ready, 4)
            pool.dma_start(wgk[112:128, :], w_gk2).then_inc(wgk_loaded, 16)
            const(gmask[:, :], "mask64", gmask_loaded)
            const(scan64[:, :], "scan64", scan64_loaded)
            pool.wait_ge(unit_used, UNITS["mlp0"])
            const(kk[0:33, 0, 0:384], "onehot", onehot_loaded, 33)
            const(flip[:, :], "flip", flip_loaded)
            wait_drained(pool, ("vec", 0))
            pool.dma_start(scratch, vt[0:16, 0:384]).then_inc(vec_stored, 16)
            pool.wait_ge(vec_stored, 16)
            hankel = bass.AP(tensor=scratch.tensor, offset=0, ap=[[1, P], [384, 16], [1, 2 * P]])
            pool.dma_start(sf[:, :].rearrange("p (h k) -> p h k", h=16), hankel).then_inc(hankel_loaded, 16)

        @block.tensor
        def _(pe):
            seen = Seen(pe, sem)

            def mm(dst, a, b, start, stop):
                return pe.matmul(dst, a, b, start=start, stop=stop)

            def mm3(dst, a, b, start, stop):
                mm(dst, a[0], b[0], start, False)
                mm(dst, a[0], b[1], False, False)
                return mm(dst, a[1], b[0], False, stop)

            def full(ins, key):
                b, _, _, unit, _, _ = FILL[key]
                ins.then_inc(bank_full[b] if unit is None else unit_used, 1)

            def weights(c, lo, n):
                return w_hi[:, c % 2, lo:lo + n], w_lo[:, c % 2, lo:lo + n]

            def tile_ready(k):
                seen.next("tile_ready")

            def xtile(k):
                return xh[:, k, :], xl[:, k, :]

            def feature_unit(stage, j, src=xtile, n=T, ready=None):
                c = UNITS[stage] + j
                pe.wait_ge(w_lo_ready, c + 1)
                for m in range(2):
                    wait_free(pe, (stage, j, m))
                for k in range(KT):
                    if ready:
                        ready(k)
                    for m in range(2):
                        last = mm3(bank((stage, j, m))[:, 0:n], weights(c, k * 256 + m * P, P), src(k), k == 0, k == KT - 1)
                        if k == KT - 1:
                            full(last, (stage, j, m))

            def token_unit(stage, j, src, tiles, n=256):
                c = UNITS[stage] + j
                pe.wait_ge(w_lo_ready, c + 1)
                per = 1 if n == P else 2
                each = tiles // per
                for m in range(per):
                    wait_free(pe, (stage, j, m))
                    for t in range(m * each, (m + 1) * each):
                        o = (t - m * each) * n
                        for k in range(KT):
                            h, l = src(k)
                            last = mm3(bank((stage, j, m))[:, o:o + n], (h[:, t * P:(t + 1) * P], l[:, t * P:(t + 1) * P]),
                                       weights(c, k * n, n), k == 0, k == KT - 1)
                    full(last, (stage, j, m))

            def layer_norm_sums(name, x_at, wait_tile, tiles=KT):
                mean_, sq_ = (name, "mean"), (name, "sq")
                seen.next("sq_used", tiles - SUMMED - 1)
                wait_free(pe, mean_)
                mm(bank(mean_)[:, :], ones[:, :], sum_x[:, :], True, False)
                wait_free(pe, sq_)
                mm(bank(sq_)[:, :], ones[:, :], sum_q[:, :], True, False)
                seen.skip("sq_ready", tiles - SUMMED)
                for k in range(tiles - SUMMED, tiles):
                    end = k == tiles - 1
                    wait_tile(k)
                    last = mm(bank(mean_)[:, :], ones[:, :], x_at(k), False, end)
                    if end:
                        full(last, mean_)
                    seen.next("sq_ready")
                    last = mm(bank(sq_)[:, :], ones[:, :], sq[:, k % 2, :], False, end)
                full(last, sq_)

            def xs_at(k):
                return xs[:, k, :]

            def residual_norm(name, keys_):
                layer_norm_sums(name, xs_at, lambda k: wait_drained(pe, keys_[k]))

            def rms_norm_sums(name, token_major=False):
                key, tok = (name, "sq"), (name, "tok")
                seen.next("sq_used", KT - SUMMED - 1)
                seen.next("sq_ready", KT)
                wait_free(pe, key)
                mm(bank(key)[:, :], ones[:, :], sum_q[:, :], True, False)
                for m in range(SUMMED):
                    last = mm(bank(key)[:, :], ones[:, :], sq[:, m, :], False, m == SUMMED - 1)
                full(last, key)
                if token_major:
                    wait_free(pe, tok)
                    for t in range(TT):
                        a = slice(t * P, (t + 1) * P)
                        mm(bank(tok)[:, t:t + 1], sum_q[:, a], ones[:, 0:1], True, False)
                        for m in range(SUMMED):
                            last = mm(bank(tok)[:, t:t + 1], sq[:, m, a], ones[:, 0:1], False, m == SUMMED - 1)
                    full(last, tok)

            def mem_src(k):
                return memh[:, k, :], meml[:, k, :]

            def filler(stage):
                for j in range(2):
                    if stage[:2] == "mk":
                        feature_unit(stage, j, mem_src, MEM)
                    else:
                        token_unit(stage, j, mem_src, MT)

            def linear_attention(name, chunk, kq, kpad, v_at, eb_kend, dv, filler):
                q, k, kend, states = kq[0], kq[1], eb_kend, kq[2]
                cpt = P // chunk
                slots = 8
                w_ = dv * P

                def unit(j):
                    if filler:
                        stage, jj = filler[j]
                        if stage == "mk0":
                            feature_unit(stage, jj, mem_src, MEM)
                        else:
                            token_unit(stage, jj, mem_src, MT)

                def square_sum(h):
                    key = (name, "ssq", h)
                    seen.next("osq_ready")
                    wait_free(pe, key)
                    for d in range(dv):
                        last = mm(bank(key)[:, :], ones[:, :], sq[:, 1 - d, :], d == 0, d == dv - 1)
                    full(last, key)

                def open_head(h):
                    seen.next("kq_ready")
                    wait_free(pe, (name, "scores", h))
                    for t in range(TT):
                        a = slice(t * P, (t + 1) * P)
                        last = mm(bank((name, "scores", h))[:, a], k[:, h, a], q[:, h, a], True, True)
                    full(last, (name, "scores", h))
                    wait_free(pe, (name, "kend", h))
                    for t in range(TT):
                        a = slice(t * P, (t + 1) * P)
                        last = pe.transpose(bank((name, "kend", h))[:, a], kend[:, a], ident[:, :])
                    full(last, (name, "kend", h))

                for h in range(HEADS):
                    open_head(h)
                    unit(2 * h)
                    if h:
                        square_sum(h - 1)
                    wait_drained(pe, (name, "scores", h))
                    wait_drained(pe, (name, "kend", h))
                    for d in range(dv):
                        wait_free(pe, (name, "o", h, d))
                        for t in range(TT):
                            a = slice(t * P, (t + 1) * P)
                            mm(bank((name, "o", h, d))[:, a], v_at(t, h * w_ + d * P, P), sum_x[:, a], t == 0, False)

                    def state_steps(t):
                        key = (name, "ds", h, t)
                        wait_free(pe, key)
                        for c in range(cpt):
                            if t * cpt + c == T // chunk - 1:
                                break
                            last = mm(bank(key)[:, c * w_:(c + 1) * w_], kpad[:, t, c * P:(c + 1) * P],
                                      v_at(t, h * w_, w_), True, True)
                        full(last, key)

                    def across_chunks(t):
                        wait_drained(pe, (name, "ds", h, t))
                        for c in range(t * cpt, (t + 1) * cpt):
                            if c == 0:
                                continue
                            a = slice(c * chunk, (c + 1) * chunk)
                            for d in range(dv):
                                s = (c % slots) * w_ + d * P
                                end = c == T // chunk - 1
                                last = mm(bank((name, "o", h, d))[:, a], states[:, s:s + P], q[:, h, a], False, end)
                                if end:
                                    full(last, (name, "o", h, d))
                        if t == 1 and filler:
                            last.then_inc(sem["inter_done"], 1)

                    if filler:
                        state_steps(0)
                        state_steps(1)
                        unit(2 * h + 1)
                        across_chunks(0)
                        state_steps(2)
                        across_chunks(1)
                        state_steps(3)
                    else:
                        for t in range(TT):
                            state_steps(t)
                        across_chunks(0)
                        across_chunks(1)
                    across_chunks(2)
                    across_chunks(3)
                square_sum(HEADS - 1)

            def queries_ahead(stage, step, steps, ready):
                for j in range(4):
                    if j >= 2:
                        step(j - 2)
                    feature_unit(stage, j, ready=ready if j == 0 else None)
                for s in range(2, steps):
                    step(s)

            def cross_attention(l):
                name = f"xa{l}"

                def step(h):
                    if h < HEADS:
                        wait_drained(pe, (f"xq{l}", h, 1))
                        for g in range(2):
                            key = (name, "s", h, g)
                            wait_free(pe, key)
                            for t in range(2):
                                for d in range(2):
                                    f = 2 * h + d
                                    last = mm(bank(key)[:, t * MEM:(t + 1) * MEM],
                                              qf[:, f, (2 * g + t) * P:(2 * g + t + 1) * P], keys[l][:, f, :], d == 0, d == 1)
                            full(last, key)
                    if h >= 2:
                        g = h - 2
                        if l == 1 and g == 0:
                            wait_drained(pe, ("mv1b", 1, 1))
                        for mt in range(MT):
                            wait_drained(pe, (name, "pT", g, mt))
                        for d in range(2):
                            key = (name, "o", g, d)
                            wait_free(pe, key)
                            for mt in range(MT):
                                v = mt * D + g * 2 * P + d * P
                                last = mm(bank(key)[:, :], values[l][:, v:v + P], pT[:, g % 2, mt, :], mt == 0, mt == 1)
                            full(last, key)
                    if 1 <= h <= HEADS:
                        g = h - 1
                        seen.next("p_ready")
                        for mt in range(MT):
                            key = (name, "pT", g, mt)
                            wait_free(pe, key)
                            for t in range(TT):
                                last = pe.transpose(bank(key)[:, t * P:(t + 1) * P],
                                                    pr[:, g % 2, t, mt * P:(mt + 1) * P], ident[:, :])
                            full(last, key)
                return step

            def chunks(name, ready):
                U, base, gate = UNITS[name], chunk_base[name], gated[name]
                hh, hl = (fhh, fhl) if gate else (mhh, mhl)
                k_ = 2 if gate else 1

                def up(tag, c, i=None, ready=None):
                    for which in ("g", "u") if gate else ("u",):
                        pe.wait_ge(w_lo_ready, at(i, per, c + 1))
                        for m in range(2):
                            wait_free(pe, (name, tag, which, m), i)
                        for k in range(KT):
                            if ready:
                                ready(k)
                            for m in range(2):
                                last = mm3(bank((name, tag, which, m))[:, :], weights(c, k * 256 + m * P, P), xtile(k),
                                           k == 0, k == KT - 1)
                                if k == KT - 1:
                                    full(last, (name, tag, which, m))
                        ready = None
                        c += 1

                def down(tag, c, chunk, i=None):
                    pe.wait_ge(w_lo_ready, at(i, per, c + 1))
                    pe.wait_ge(sem["h_ready"], at(i, 4, 2 * (base + chunk) + 2))
                    for m in range(KT):
                        key = (name, tag, "d", m)
                        wait_free(pe, key, i)
                        for k in range(2):
                            last = mm3(bank(key)[:, :], weights(c, k * D + m * P, P),
                                       (hh[:, chunk % 2, k, :], hl[:, chunk % 2, k, :]), k == 0, k == 1)
                        full(last, key)

                per = 2 * (k_ + 1)
                trips = LOOP_TRIPS[gate]
                up("first", U, ready=ready)
                c = U + k_
                with pe.Fori(0, trips) as i:
                    up(0, c, i)
                    down(0, c + k_, 0, i)
                    up(1, c + k_ + 1, i)
                    down(1, c + 2 * k_ + 1, 1, i)
                c += trips * per
                if not gate:
                    up("late", c)
                    down("late", c + k_, 2 * trips)
                    c += k_ + 1
                down("last", c, 2 * trips + (0 if gate else 1))

            feature_unit("ag0", 0, ready=tile_ready)
            feature_unit("a0", 0)
            feature_unit("ag1", 0)
            feature_unit("f", 0)
            feature_unit("f", 1)
            pe.wait_ge(ones_ready, 3)
            seen.next("memsq_ready")
            for key, src in ((("memn", "mean"), mk[:, :, :]), (("memn", "sq"), mv[:, :].rearrange("p (k t) -> p k t", k=KT))):
                wait_free(pe, key)
                for k in range(KT):
                    last = mm(bank(key)[:, 0:MEM], ones[:, :], src[:, k, :], k == 0, k == KT - 1)
                full(last, key)
            feature_unit("g", 0)
            feature_unit("g", 1)
            feature_unit("a1", 0)
            feature_unit("q", 0)
            feature_unit("q", 1)
            token_unit("v", 0, xtile, TT)
            token_unit("v", 1, xtile, TT)
            pe.wait_ge(ident_loaded, 16)
            seen.next("mem_ready")
            wait_drained(pe, ("v", 1, 1))
            linear_attention("hg", 32, (hq, hk, hs), kend_hg, lambda t, c, n: hv[:, t, c:c + n], henb, 1, HG_FILLER)

            def mixed_ready(k):
                if k == 3:
                    layer_norm_sums("cvn", lambda k: cacc[:, k, :], lambda k: pe.wait_ge(sem["conv_ready"], k + 1), 4)
                tile_ready(k)

            for j in range(4):
                feature_unit("mixo", j, ready=mixed_ready if j == 0 else None)
            residual_norm("mixn0", pair_keys("mixo"))

            for l in range(2):
                filler(FILLER[f"mixn{l}"])
                wait_drained(pe, ("mv0", 3, 1) if l == 0 else ("mk1b", 1, 1))
                queries_ahead(f"xq{l}", cross_attention(l), HEADS + 2, tile_ready)
                for j in range(4):
                    feature_unit(f"xo{l}", j, ready=(lambda k: wait_drained(pe, (f"xa{l}", "o", k // 2, k % 2))) if j == 0 else None)
                residual_norm(f"xan{l}", pair_keys(f"xo{l}"))
                if l == 0:
                    filler(FILLER["xan0"])
                chunks(f"ffn{l}", tile_ready)
                residual_norm(f"ffnn{l}", last_down_keys(f"ffn{l}"))
                if l == 0:
                    filler(FILLER["ffnn0"])
                    c = UNITS["pool"]
                    pe.wait_ge(w_lo_ready, c + 1)
                    for m in range(KT):
                        g = m // 2
                        if m % 2 == 0:
                            seen.next("tile_ready", 2)
                        wait_free(pe, ("pool", 0, m))
                        for k in range(2):
                            last = mm3(bank(("pool", 0, m))[:, :], weights(c, (2 * g + k) * 256 + (m % 2) * P, P),
                                       xtile(2 * g + k), k == 0, k == 1)
                        full(last, ("pool", 0, m))
                    residual_norm("mixn1", [("pool", 0, m) for m in range(KT)])

            c = UNITS["glr"]
            pe.wait_ge(w_lo_ready, c + 1)
            wait_free(pe, ("glr", 0, 0))
            for k in range(KT):
                tile_ready(k)
                last = mm3(bank(("glr", 0, 0))[:, :], weights(c, k * P, P), xtile(k), k == 0, k == KT - 1)
            full(last, ("glr", 0, 0))
            feature_unit("gq", 0, ready=lambda k: rms_norm_sums("r0", True) if k == 2 else None)
            feature_unit("gq", 1)
            wait_drained(pe, ("glr", 0, 0))
            pe.wait_ge(wgk_loaded, 16)
            for h in range(HEADS):
                wait_free(pe, ("gkz", h))
                full(mm(bank(("gkz", h))[:, :], wgk[96:128, h * P:(h + 1) * P], glow[96:128, :], True, True), ("gkz", h))
            feature_unit("gk", 0)
            feature_unit("gk", 1)
            for j in range(4):
                feature_unit("gg", j)
            for j in range(4):
                token_unit("gv", j, xtile, TT)
            linear_attention("gla", 64, (gq, gk, gs), kend_gla, lambda t, c, n: gv[:, t, c:c + n], genb, 2, None)
            for j in range(4):
                feature_unit("go", j, ready=tile_ready if j == 0 else None)
            pe.wait_ge(onehot_loaded, 16)
            pe.wait_ge(table_loaded, 16)
            wait_free(pe, ("vec", 0))
            full(mm(bank(("vec", 0))[0:16, 0:384], tab[:, :], kk[0:33, 0, 0:384], True, True), ("vec", 0))
            def tile_and_sums(name):
                def ready(k):
                    tile_ready(k)
                    if k == 2:
                        rms_norm_sums(name)
                return ready

            chunks("mlp0", tile_and_sums("r1"))
            pe.wait_ge(hankel_loaded, 16)
            pe.wait_ge(flip_loaded, 16)
            def bias_tile(m):
                wait_free(pe, ("bias", m))
                full(mm(bank(("bias", m))[:, :], flip[:, :], sf[:, m * T:(m + 1) * T], True, True), ("bias", m))

            def kv_ready(k):
                tile_ready(k)
                if k == 3:
                    rms_norm_sums("r2", True)

            bias_tile(0)
            bias_tile(1)
            ytile = lambda k: (yh[:, k, :], yl[:, k, :])
            feature_unit("sk", 0, ytile, ready=kv_ready)
            for m in range(2, 8):
                bias_tile(m)
            token_unit("sv", 0, ytile, TT, P)
            qv = sf[:, :].rearrange("p (k t) -> p k t", k=KT)

            def swa(it):
                if it == 0:
                    wait_drained(pe, ("sk", 0, 1))
                if it == 2:
                    wait_drained(pe, ("sv", 0, 0))
                if it < SWA_ITEMS:
                    hp, nn = it // 2, it % 2
                    if nn == 0:
                        wait_drained(pe, ("sq", hp // 2, 1))
                    for j in range(2):
                        key = ("swa", "s", it, j)
                        wait_free(pe, key)
                        r = slice(64 * j, 64 * j + 64)
                        for n in range(2):
                            blk = 2 * nn + n
                            lo = max(blk - 1, 0) * P
                            wd = (blk + 1) * P - lo
                            last = mm(bank(key)[:, (n + 1) * 256 - wd:(n + 1) * 256], qv[r, hp, blk * P:(blk + 1) * P],
                                      kk[r, hp // 4, lo:lo + wd], True, True)
                        full(last, key)
                if it >= 2:
                    g = it - 2
                    hp, nn = g // 2, g % 2
                    key = ("swa", "o", hp)
                    if nn == 0:
                        wait_free(pe, key)
                    for j in range(2):
                        wait_drained(pe, ("swa", "pT", g, j))
                        for n in range(2):
                            blk = 2 * nn + n
                            for kt in range(2):
                                if blk + kt == 0:
                                    continue
                                v = (blk - 1 + kt) * P + (hp // 4) * 64
                                last = mm(bank(key)[64 * j:64 * j + 64, blk * P:(blk + 1) * P], vt[:, v:v + 64],
                                          spT[:, g % 2, j, (2 * n + kt) * P:(2 * n + kt + 1) * P],
                                          kt == 0 or blk == 0, kt == 1)
                    if nn == 1:
                        full(last, key)
                if 1 <= it <= SWA_ITEMS:
                    g = it - 1
                    nn = g % 2
                    for j in range(2):
                        key = ("swa", "pT", g, j)
                        seen.next("p_ready")
                        wait_free(pe, key)
                        pv = mh[:, g % 2, j, :]
                        for s_ in range(1 if nn == 0 else 0, 4):
                            last = pe.transpose(bank(key)[:, s_ * P:(s_ + 1) * P], pv[:, s_ * P:(s_ + 1) * P], ident[:, :])
                        full(last, key)

            queries_ahead("sq", swa, SWA_ITEMS + 2, tile_ready)
            for j in range(4):
                feature_unit("so", j, ready=(lambda k: wait_drained(pe, ("swa", "o", k))) if j == 0 else None)
            chunks("mlp1", tile_and_sums("r3"))
            rms_norm_sums("fin")

        @block.scalar
        def _(act):
            seen = Seen(act, sem)
            steps = Tally(act, act_steps)

            def give(ins, name):
                ins.then_inc(sem[name], 1)

            def split_hi(c, i=None, per=0):
                if c >= N_UNITS:
                    return
                act.wait_ge(raw_loaded[c % 2], at(i, 8 * per, 16 * (c // 2 + 1)))
                if c >= 2:
                    act.wait_ge(unit_used, at(i, per, c - 1))
                act.activation(w_hi[:, c % 2, :], w_raw[:, c % 2, :], ACT.Copy).then_inc(w_hi_ready, 1)

            def drain(key, dst, src, func=ACT.Copy, i=None, **kw):
                wait_full(act, key, i)
                free(act.activation(dst, src, func, **kw), key)

            def drain_pair(stage, j, dst, n=T, func=ACT.Copy, **kw):
                for m in range(2):
                    drain((stage, j, m), dst(m), bank((stage, j, m))[:, 0:n], func, **kw)

            def high(k, src, scale=None, dst=None):
                kw = {} if scale is None else {"scale": scale}
                give(act.activation((xh if dst is None else dst)[:, k, :], src, ACT.Copy, **kw), "x_hi")

            def square(k, src):
                if k == 2 or k >= 4:
                    seen.next("sq_used")
                give(act.activation(sq[:, k % 2, :], src, ACT.Square), "sq_ready")

            def inverse_root(dst, name):
                steps.step(act.activation(dst, dst, ACT.Ln))
                steps.wait()
                give(act.activation(dst, dst, ACT.Exp, scale=-0.5), name)

            def mean_stats(name, n, count=T, split=None):
                if split:
                    split_hi(split)
                key = (name, "mean")
                drain(key, mean[:, 0:count], bank(key)[:, 0:count], scale=1.0 / n)
                wait_drained(act, key)
                give(act.activation(rstd[:, 0:count], mean[:, 0:count], ACT.Square), "msq_ready")
                seen.next("var_ready")
                inverse_root(rstd[:, 0:count], "rstd_ready")

            def rms_stats(name):
                wait_drained(act, (name, "sq"))
                inverse_root(rstd[:, :], "rstd_ready")

            def apply_norm(param, l, then, n, stage=None):
                def copy_out(j):
                    if stage[:2] == "mk":
                        f = 4 * "ab".index(stage[3]) + 2 * j
                        drain_pair(stage, j, lambda m: mk1[:, f + m, :], MEM)
                    else:
                        f = 512 * "ab".index(stage[3]) + 256 * j
                        drain_pair(stage, j, lambda m: mv1[:, m * D + f:m * D + f + 256], MEM)

                for k in range(KT):
                    if stage is None:
                        if k == 4:
                            split_hi(n + 1)
                    elif k in (1, 4):
                        copy_out(k // 3)
                        split_hi(n + 2 + k // 3)
                    seen.next("zn_ready")
                    give(act.activation(xs[:, k, :], xs[:, k, :], ACT.Identity, scale=col(f"{param}_g{l}", k),
                                        bias=col(f"{param}_b{l}", k)), "xn_ready")
                    then(k)

            def behind(name):
                return UNITS[FILLER[name]] + 1 if name in FILLER else None

            xn_made = [0]

            def own_xn():
                xn_made[0] += 1
                act.wait_ge(sem["xn_ready"], xn_made[0])

            def high_of_xs(k):
                own_xn()
                high(k, xs[:, k, :])

            def residual(keys, c0, n_units, norm, n=D, first=0):
                for j in range(n_units):
                    if j >= first:
                        split_hi(c0 + j + 1)
                    for m in range(2):
                        k = 2 * j + m
                        wait_drained(act, keys[k])
                        square(k, xs[:, k, :])
                if norm:
                    mean_stats(norm, n, split=behind(norm))

            def late_high(gain, l, last_key):
                wait_full(act, last_key)
                for k in range(KT):
                    high(k, xs[:, k, :], col(f"{gain}_g{l}" if l is not None else gain, k))

            def chunks(name, final_squares=True):
                U, base, gate = UNITS[name], chunk_base[name], gated[name]
                hid, hh = (fh, fhh) if gate else (mh, mhh)
                k_ = 2 if gate else 1
                per = 2 * (k_ + 1)
                trips = LOOP_TRIPS[gate]

                def up(tag, c, chunk, i=None):
                    if not (gate and tag == "first"):
                        split_hi(c + 1, i, per)
                    if gate:
                        for m in range(2):
                            key = (name, tag, "g", m)
                            drain(key, sil[:, m, :], bank(key)[:, :], ACT.Silu, i)
                        split_hi(c + 2, i, per)
                    for m in range(2):
                        if gate:
                            wait_drained(act, (name, tag, "u", m), i)
                            src = hid[:, m, :]
                        else:
                            act.wait_ge(sem["hf_ready"], at(i, 4, 2 * (base - 2 * FFN_CHUNKS + chunk) + m + 1))
                            src = hid[:, chunk % 2, m, :]
                        give(act.activation(hh[:, chunk % 2, m, :], src, ACT.Copy), "hh_ready")

                def down(c, i=None):
                    split_hi(c + 1, i, per)

                up("first", U, 0)
                c = U + k_
                with act.Fori(0, trips) as i:
                    up(0, c, 1, i)
                    down(c + k_, i)
                    up(1, c + k_ + 1, 2, i)
                    down(c + 2 * k_ + 1, i)
                c += trips * per
                if not gate:
                    up("late", c, 2 * trips + 1)
                    down(c + k_)
                    c += k_ + 1
                down(c)
                for k in range(KT):
                    wait_drained(act, (name, "last", "d", k))
                    square(k, xs[:, k, :])

            def linear_attention(name, chunk, b_, eb, kend, kpad, scale, dv, out_tile, filler):
                def prepare(h):
                    if h == 0:
                        seen.next("b_ready", HEADS)
                    if h:
                        seen.next("kq_ready")
                        wait_full(act, (name, "kend", h - 1))
                    give(act.activation(eb[:, :], b_[:, h, :], ACT.Exp, scale=scale), "eb_ready")
                    give(act.activation(kend[:, :], b_[:, h, :], ACT.Exp, scale=-scale), "eb_ready")

                def unit(j):
                    if filler:
                        stage, jj = filler[j]
                        c = UNITS[stage] + jj
                        split_hi(c + 1)
                        if stage == "mk0":
                            drain_pair(stage, jj, lambda m: mk[:, 2 * jj + m, :], MEM)
                        else:
                            drain_pair(stage, jj, lambda m: mv[:, m * D + jj * 256:m * D + (jj + 1) * 256], MEM)

                def finish(h):
                    wait_drained(act, (name, "ssq", h))
                    inverse_root(rstd[:, :], "rstd_ready")

                def outputs(h):
                    for d in range(dv):
                        seen.next("y_ready")
                        high(dv * h + d, out_tile(h, d))

                prepare(0)
                seen.next("kpad_ready")
                for h in range(HEADS):
                    key = (name, "kend", h)
                    wait_full(act, key)
                    for c in range(P // chunk):
                        r = slice(c * chunk, (c + 1) * chunk)
                        last = act.activation(kpad[r, :, c * P:(c + 1) * P],
                                              bank(key)[r, :].rearrange("p (t n) -> p t n", t=TT), ACT.Copy)
                    free(last, key)
                    unit(2 * h)
                    if h:
                        finish(h - 1)
                    if h + 1 < HEADS:
                        prepare(h + 1)
                    else:
                        seen.next("kq_ready")
                    if h and filler:
                        outputs(h - 1)
                    unit(2 * h + 1)
                    for d in range(dv):
                        drain((name, "o", h, d), out_tile(h, d), bank((name, "o", h, d))[:, :])
                    for d in range(dv):
                        wait_drained(act, (name, "o", h, d))
                        last = act.activation(sq[:, 1 - d, :], out_tile(h, d), ACT.Square)
                        if d == dv - 1:
                            give(last, "osq_ready")
                    if h and not filler:
                        outputs(h - 1)
                finish(HEADS - 1)
                outputs(HEADS - 1)

            def queries_ahead(split, drain_unit, step, steps):
                for j in range(4):
                    split(j)
                    if j >= 2:
                        step(j - 2)
                    drain_unit(j)
                for s in range(2, steps):
                    step(s)

            def cross_attention(l):
                name = f"xa{l}"

                def step(h):
                    if h < HEADS:
                        seen.next("rowmax_ready")
                        for t in range(TT):
                            key = (name, "s", h, t // 2)
                            last = act.activation(pr[:, h % 2, t, :], bank(key)[:, (t % 2) * MEM:(t % 2 + 1) * MEM], ACT.Exp,
                                                  bias=rmax[:, h % 2, t:t + 1], accum_out=rsum[:, h % 2, t:t + 1])
                            if t % 2:
                                free(last, key)
                    if h >= 2:
                        for d in range(2):
                            key = (name, "o", h - 2, d)
                            wait_full(act, key)
                            high(2 * (h - 2) + d, bank(key)[:, :])
                    if 1 <= h <= HEADS:
                        key = (name, "pT", h - 1, 0)
                        drain(key, pT[:, (h - 1) % 2, 0, :], bank(key)[:, :])
                return step

            act.wait_ge(x_loaded[0], 16)
            for k in range(2):
                high(k, xs[:, k, :])
            split_hi(0)
            for k in range(2, KT):
                if k % 2 == 0:
                    act.wait_ge(x_loaded[k // 2], 16)
                high(k, xs[:, k, :])
            seen.next("lbd_ready")
            give(act.activation(lbs[:, :, :], lbs[:, :, :], ACT.Exp), "lbe_ready")
            sga = hs[:, :].rearrange("p (m t) -> p m t", m=2)
            U = UNITS["ag0"]
            split_hi(U + 1)
            drain_pair("ag0", 0, lambda m: sga[:, m, :], func=ACT.Sigmoid)
            split_hi(U + 2)
            split_hi(U + 3)
            drain_pair("ag1", 0, lambda m: cacc[:, 2 + m, :], func=ACT.Sigmoid)
            act.wait_ge(mem_loaded, 16)
            give(act.activation(mv[:, :], mk[:, :, :].rearrange("p k t -> p (k t)"), ACT.Square), "memsq_ready")
            for j in range(2):
                split_hi(UNITS["f"] + j + 1)
                for m in range(2):
                    key, h = ("f", j, m), 2 * j + m
                    wait_full(act, key)
                    act.activation(hb[:, h, :], bank(key)[:, :], ACT.Sigmoid)
                    free(act.activation(hk[:, h, :], bank(key)[:, :], ACT.Sigmoid, scale=-1.0), key)
            for j in range(2):
                split_hi(UNITS["g"] + j + 1)
                for m in range(2):
                    key = ("g", j, m)
                    wait_full(act, key)
                    give(act.activation(hg[:, 2 * j + m, :], bank(key)[:, :], ACT.Sigmoid), "gate_ready")
            split_hi(UNITS["a1"] + 1)
            act.preload_act_table_set("natural_log_exp_and_others")
            mean_stats("memn", D, MEM)
            split_hi(UNITS["q"] + 1)
            drain_pair("q", 0, lambda m: hq[:, m, :])
            for k in range(KT):
                seen.next("memz_ready") if k == 0 else None
                last = act.activation(mk[:, k, :], mk[:, k, :], ACT.Identity, scale=col("mem_g", k), bias=col("mem_b", k))
            steps.step(last)
            steps.wait()
            give(act.activation(memh[:, :, :].rearrange("p k t -> p (k t)"), mk[:, :, :].rearrange("p k t -> p (k t)"), ACT.Copy), "memn_ready")
            split_hi(UNITS["q"] + 2)
            drain_pair("q", 1, lambda m: hq[:, 2 + m, :])
            seen.next("f_ready", HEADS)
            for h in range(HEADS):
                give(act.activation(hb[:, h, :], hb[:, h, :], ACT.Ln), "logf_ready")
            for j in range(2):
                split_hi(UNITS["v"] + j + 1)
                for m in range(2):
                    key = ("v", j, m)
                    drain(key, hv[:, 2 * m:2 * m + 2, j * 256:(j + 1) * 256], bank(key)[:, :].rearrange("p (t n) -> p t n", t=2))
            linear_attention("hg", 32, hb, heb, henb, kend_hg, 1.0, 1, lambda h, d: hq[:, h, :], HG_FILLER)
            for k in range(4):
                seen.next("conv_ready")
                square(k, cacc[:, k, :])
            mean_stats("cvn", 512)
            for k in range(4):
                if k == 2:
                    split_hi(UNITS["mixo"] + 1)
                seen.next("zn_ready")
                steps.step(act.activation(cacc[:, k, :], cacc[:, k, :], ACT.Silu, scale=col("cv_g", k), bias=col("cv_lb", k)))
                steps.wait()
                high(4 + k, cacc[:, k, :])
            residual(pair_keys("mixo"), UNITS["mixo"], 4, None, first=1)
            for l in range(2):
                act.preload_act_table_set("natural_log_exp_and_others")
                mean_stats(f"mixn{l}", D, split=behind(f"mixn{l}"))
                stage = FILLER[f"mixn{l}"]
                apply_norm("mix", l, high_of_xs, UNITS[stage], stage)
                queries_ahead(lambda j: j and split_hi(UNITS[f"xq{l}"] + j + 1),
                              lambda j: drain_pair(f"xq{l}", j, lambda m: qf[:, 2 * j + m, :], scale=0.0625),
                              cross_attention(l), HEADS + 2)
                residual(pair_keys(f"xo{l}"), UNITS[f"xo{l}"], 4, f"xan{l}")

                stage = FILLER.get(f"xan{l}")
                apply_norm("xa", l, high_of_xs, UNITS[stage or f"ffn{l}"], stage)
                act.preload_act_table_set("silu_and_others")
                chunks(f"ffn{l}")
                act.preload_act_table_set("natural_log_exp_and_others")
                mean_stats(f"ffnn{l}", D, split=behind(f"ffnn{l}"))
                if l == 0:
                    def pool_input(k):
                        own_xn()
                        give(act.activation(pa[:, k, PAD:], xs[:, k, :], ACT.Copy), "x_hi")
                        if k >= 2 and k % 2 == 0:
                            pooled(k // 2 - 1)

                    def pooled(g):
                        for k in (2 * g, 2 * g + 1):
                            seen.next("pool_ready")
                            high(k, pp[:, k, :])
                            give(act.activation(xs[:, k, :], xs[:, k, :], ACT.Copy, scale=ALPHA), "scaled")

                    apply_norm("ffn", 0, pool_input, UNITS[FILLER["ffnn0"]], FILLER["ffnn0"])
                    pooled(3)
                    for k in range(KT):
                        wait_drained(act, ("pool", 0, k))
                        square(k, xs[:, k, :])

            def first_rms(k):
                own_xn()
                high(k, xs[:, k, :], col("mix2_g0", k))
                square(k, xs[:, k, :])

            apply_norm("ffn", 1, first_rms, UNITS["glr"])
            rms_stats("r0")
            seen.next("tok_ready")
            inverse_root(rtok[:, :], "rtok_ready")
            for j in range(2):
                split_hi(UNITS["gq"] + j + 1)
            for h in range(HEADS):
                z = gb[:, h, :]
                wait_drained(act, ("gkz", h))
                t = sq[:, h % 2, :]
                if h >= 2:
                    act.wait_ge(sem["z_ready"], h - 1)
                steps.step(act.activation(t, z, ACT.Abs))
                steps.wait()
                steps.step(act.activation(t, t, ACT.Exp, scale=-1.0))
                steps.wait()
                give(act.activation(t, t, ACT.Ln, bias=ones[:, 0:1]), "lsig_ready")
            for j in range(2):
                split_hi(UNITS["gk"] + j + 1)
            for j in range(4):
                split_hi(UNITS["gg"] + j + 1)
                for m in range(2):
                    wait_drained(act, ("gg", j, m))
                    last = act.activation(gg[:, 2 * j + m, :], gg[:, 2 * j + m, :], ACT.Silu)
            give(last, "gate_ready")
            act.preload_act_table_set("natural_log_exp_and_others")
            seen.next("rtok_ready")
            for j in range(4):
                split_hi(UNITS["gv"] + j + 1)
                for m in range(2):
                    key = ("gv", j, m)
                    wait_full(act, key)
                    for t in range(2):
                        tt = 2 * m + t
                        last = act.activation(gv[:, tt, j * 256:(j + 1) * 256], bank(key)[:, t * 256:(t + 1) * 256], ACT.Copy,
                                              scale=rtok[:, tt:tt + 1])
                    free(last, key)
            linear_attention("gla", 64, gb, geb, genb, kend_gla, 1.0 / 16.0, 2, lambda h, d: mh[:, h % 2, d, :], None)
            residual(pair_keys("go"), UNITS["go"], 4, None)
            late_high("mlp2", 0, ("go", 3, 1))
            rms_stats("r1")
            chunks("mlp0")
            wait_full(act, ("mlp0", "last", "d", KT - 1))
            for k in range(KT):
                high(k, xs[:, k, :], col("kvn", k), yh)

            def drain_bias(m):
                key = ("bias", m)
                drain(key, bias[:, 2 * m:2 * m + 2, :], bank(key)[:, :].rearrange("p (h k) -> p h k", h=2))

            drain_bias(0)
            drain_bias(1)
            rms_stats("r2")
            seen.next("tok_ready")
            inverse_root(rtok[:, :], "rtok_ready")
            high(0, xs[:, 0, :], col("mix2_g1", 0))
            high(1, xs[:, 1, :], col("mix2_g1", 1))
            split_hi(UNITS["sk"] + 1)
            for k in range(2, KT):
                drain_bias(k)
                high(k, xs[:, k, :], col("mix2_g1", k))
            split_hi(UNITS["sv"] + 1)
            seen.next("rtok_ready")
            key = ("sv", 0, 0)
            wait_full(act, key)
            for t in range(TT):
                last = act.activation(vt[:, t * P:(t + 1) * P], bank(key)[:, t * P:(t + 1) * P], ACT.Copy, scale=rtok[:, t:t + 1])
            free(last, key)

            def swa(it):
                if it < SWA_ITEMS:
                    hp, nn = it // 2, it % 2
                    for j in range(2):
                        seen.next("rowmax_ready")
                        for n in range(2):
                            lo = P if 2 * nn + n == 0 else 0
                            s_ = mh[:, it % 2, j, n * 256 + lo:(n + 1) * 256]
                            act.activation(s_, s_, ACT.Exp, bias=rmax[:, it % 2, 2 * j + n:2 * j + n + 1],
                                           accum_out=rsum[:, it % 2, 2 * j + n:2 * j + n + 1])
                        h = 2 * hp + j
                        give(act.activation(rsnk[:, it % 2, 2 * j:2 * j + 2], rmax[:, it % 2, 2 * j:2 * j + 2], ACT.Exp,
                                            bias=skb[:, h:h + 1]), "e_ready")
                if it >= 2 and it % 2:
                    hp = (it - 2) // 2
                    key = ("swa", "o", hp)
                    wait_full(act, key)
                    high(hp, bank(key)[:, :])
                if 1 <= it <= SWA_ITEMS:
                    g = it - 1
                    lo = P if g % 2 == 0 else 0
                    for j in range(2):
                        key = ("swa", "pT", g, j)
                        drain(key, spT[:, g % 2, j, lo:T], bank(key)[:, lo:T])

            queries_ahead(lambda j: split_hi(UNITS["sq"] + j + 1), lambda j: None, swa, SWA_ITEMS + 2)
            residual(pair_keys("so"), UNITS["so"], 4, None)
            late_high("mlp2", 1, ("so", 3, 1))
            rms_stats("r3")
            chunks("mlp1")
            rms_stats("fin")

        @block.vector
        def _(dve):
            seen = Seen(dve, sem)
            steps = Tally(dve, dve_steps)
            made = {}

            def give(ins, name):
                ins.then_inc(sem[name], 1)
                made[name] = made.get(name, 0) + 1

            def own(name):
                dve.wait_ge(sem[name], made[name])

            def split_lo(c, i=None, per=0):
                if c >= N_UNITS:
                    return
                dve.wait_ge(w_hi_ready, at(i, per, c + 1))
                dve.tensor_tensor(w_lo[:, c % 2, :], w_raw[:, c % 2, :], w_hi[:, c % 2, :].bitcast(F32), ALU.subtract)\
                   .then_inc(w_lo_ready, 1)

            def rest(k, src, gain=None, hi=None, lo=None):
                h, l = (xh if hi is None else hi)[:, k, :].bitcast(F32), (xl if lo is None else lo)[:, k, :]
                seen.next("x_hi")
                if gain is None:
                    return dve.tensor_tensor(l, src, h, ALU.subtract)
                return dve.scalar_tensor_tensor(l, src, gain, h, ALU.mult, ALU.subtract)

            def add_to_sums(k, has_mean, x_at, tiles=KT):
                if k == 0 or k >= tiles - SUMMED:
                    return
                seen.next("sq_ready", 2 if k == 1 else 1)
                if has_mean:
                    if k > 1:
                        dve.wait_ge(dve_steps, sum_step[0])
                    sum_step[0] = steps.step(dve.tensor_tensor(sum_x[:, :], x_at(0) if k == 1 else sum_x[:, :], x_at(k), ALU.add))
                if k > 1:
                    own("sq_used")
                give(dve.tensor_tensor(sum_q[:, :], sq[:, 0, :] if k == 1 else sum_q[:, :], sq[:, k % 2, :], ALU.add), "sq_used")
                if k == tiles - SUMMED - 1:
                    seen.skip("sq_ready", SUMMED)

            sum_step = [0]

            def xs_at(k):
                return xs[:, k, :]

            def residual(keys, c0, n_units, has_mean, alpha=None, first=0):
                for j in range(n_units):
                    if first <= j < n_units - 1:
                        split_lo(c0 + j + 1)
                    for m in range(2):
                        k = 2 * j + m
                        add(k, keys[k], alpha)
                        sums_behind(k, keys, has_mean)
                split_lo(c0 + n_units)

            def sums_behind(k, keys, has_mean):
                if 2 <= k < KT - SUMMED + 1:
                    wait_drained(dve, keys[k - 1])
                    add_to_sums(k - 1, has_mean, xs_at)

            def add(k, key, alpha=None, i=None):
                wait_full(dve, key, i)
                if alpha is None:
                    free(dve.tensor_tensor(xs[:, k, :], xs[:, k, :], bank(key)[:, :], ALU.add), key)
                else:
                    free(dve.scalar_tensor_tensor(xs[:, k, :], xs[:, k, :], alpha, bank(key)[:, :], ALU.mult, ALU.add), key)

            def variance(name, n, count=T):
                key = (name, "sq")
                wait_full(dve, key)
                seen.next("msq_ready")
                r = rstd[:, 0:count]
                free(dve.scalar_tensor_tensor(r, bank(key)[:, 0:count], 1.0 / n, r, ALU.mult, ALU.subtract), key)
                wait_drained(dve, key)
                give(dve.tensor_scalar(r, r, 0.0, LN_EPS, ALU.max, ALU.add), "var_ready")

            def mean_square(key, n):
                wait_full(dve, key)
                free(dve.tensor_scalar(rstd[:, :], bank(key)[:, :], 1.0 / n, RMS_EPS, ALU.mult, ALU.add), key)

            def token_rstd(name):
                key = (name, "tok")
                wait_full(dve, key)
                free(dve.tensor_scalar(rtok[:, :], bank(key)[:, 0:TT], 1.0 / D, RMS_EPS, ALU.mult, ALU.add), key)
                wait_drained(dve, key)
                give(dve.tensor_copy(rtok[:, :], rtok[:, :]), "tok_ready")

            def normalise(name, n, x_at, tiles, then, unit=None, stage=None):
                centred = {}

                def centre(k):
                    centred[k] = steps.step(dve.tensor_tensor(x_at(k), x_at(k), mean[:, :], ALU.subtract))

                wait_drained(dve, (name, "mean"))
                centre(0)
                variance(name, n)
                for k in range(1, 4):
                    centre(k)
                if stage:
                    split_lo(unit + 1)
                seen.next("rstd_ready")
                for k in range(tiles):
                    if stage and k == 2:
                        split_lo(unit + 2)
                    steps.wait(centred[k])
                    give(dve.tensor_tensor(x_at(k), x_at(k), rstd[:, :], ALU.mult), "zn_ready")
                    if k + 4 < tiles:
                        centre(k + 4)
                    if k:
                        then(k - 1)
                then(tiles - 1)
                split_lo(unit + 3 if stage else unit + 1)

            def rest_of_xs(k):
                seen.skip("xn_ready", 1)
                give(rest(k, xs[:, k, :]), "tile_ready")

            def scale_residual():
                for k in range(KT):
                    last = dve.tensor_scalar(xs[:, k, :], xs[:, k, :], ALPHA, None, ALU.mult)
                steps.step(last)
                steps.wait()

            def late_rest(gain, l):
                for k in range(KT):
                    give(rest(k, xs[:, k, :], col(f"{gain}_g{l}", k)), "tile_ready")

            def chunks(name, has_mean):
                U, base, gate = UNITS[name], chunk_base[name], gated[name]
                hid, hh, hl = (fh, fhh, fhl) if gate else (mh, mhh, mhl)
                k_ = 2 if gate else 1
                per = 2 * (k_ + 1)
                trips = LOOP_TRIPS[gate]

                def up(tag, c, chunk, i=None):
                    if not (gate and tag == "first"):
                        split_lo(c + 1, i, per)
                    if gate:
                        split_lo(c + 2, i, per)
                        if tag == "first":
                            scale_residual()
                    for m in range(2):
                        key = (name, tag, "u", m)
                        wait_full(dve, key, i)
                        if gate:
                            wait_drained(dve, (name, tag, "g", m), i)
                            free(dve.tensor_tensor(hid[:, m, :], sil[:, m, :], bank(key)[:, :], ALU.mult), key)
                        else:
                            free(dve.tensor_tensor(hid[:, chunk % 2, m, :], bank(key)[:, :], rstd[:, :], ALU.mult), key)
                    if not gate:
                        for m in range(2):
                            h = hid[:, chunk % 2, m, :]
                            wait_drained(dve, (name, tag, "u", m), i)
                            dve.scalar_tensor_tensor(h, h, 0.0, h, ALU.max, ALU.mult).then_inc(sem["hf_ready"], 1)
                    for m in range(2):
                        h = hid[:, m, :] if gate else hid[:, chunk % 2, m, :]
                        dve.wait_ge(sem["hh_ready"], at(i, 4, 2 * (base + chunk) + m + 1))
                        dve.tensor_tensor(hl[:, chunk % 2, m, :], h, hh[:, chunk % 2, m, :].bitcast(F32), ALU.subtract)\
                           .then_inc(sem["h_ready"], 1)

                def down(tag, c, i=None):
                    for m in range(KT):
                        if m == 2:
                            split_lo(c + 1, i, per)
                        add(m, (name, tag, "d", m), i=i)

                up("first", U, 0)
                c = U + k_
                with dve.Fori(0, trips) as i:
                    up(0, c, 1, i)
                    down(0, c + k_, i)
                    up(1, c + k_ + 1, 2, i)
                    down(1, c + 2 * k_ + 1, i)
                c += trips * per
                if not gate:
                    up("late", c, 2 * trips + 1)
                    down("late", c + k_)
                    c += k_ + 1
                keys = last_down_keys(name)
                for k in range(KT):
                    add(k, keys[k])
                    sums_behind(k, keys, has_mean)
                split_lo(c + 1)

            def conv_taps(pair):
                done = [0, 0]
                for j in range(TAPS):
                    for m in range(2):
                        ct = 2 * pair + m
                        a, u = cacc[:, ct, :], cu[:, m, j:j + T]
                        wj = col("cv_w", ct * TAPS + j)
                        if j == 0:
                            ins = dve.tensor_scalar(a, u, wj, col("cv_b", ct), ALU.mult, ALU.add)
                        else:
                            dve.wait_ge(dve_steps, done[m])
                            ins = dve.scalar_tensor_tensor(a, u, wj, a, ALU.mult, ALU.add)
                        if j < TAPS - 1:
                            done[m] = steps.step(ins)
                        else:
                            give(ins, "conv_ready")
                        yield

            conv = {"it": iter(())}

            def taps(n):
                for _ in range(n):
                    if next(conv["it"], 0) == 0:
                        return

            def linear_attention(name, chunk, q, k, b_, eb, kend, mask, states, dv, out_tile, gate_at, gain_at, filler, after_first=None):
                cpt = P // chunk
                nch = T // chunk
                slots = 8
                w_ = dv * P
                def prepare(h):
                    dec = hdec[:, h % 2, 0:nch]
                    seen.next("eb_ready", 2)
                    dve.tensor_tensor(q[:, h, :], q[:, h, :], eb[:, :], ALU.mult)
                    steps.step(dve.tensor_copy(dec, eb[:, :].rearrange("p (c t) -> p c t", t=chunk)[:, :, chunk - 1]))
                    steps.step(dve.tensor_tensor(k[:, h, :], k[:, h, :], kend[:, :], ALU.mult))
                    steps.wait()
                    give(dve.tensor_tensor(kend[:, :].rearrange("p (c t) -> p c t", t=chunk),
                                           k[:, h, :].rearrange("p (c t) -> p c t", t=chunk),
                                           dec.unsqueeze(2).broadcast_to([P, nch, chunk]), ALU.mult), "kq_ready")

                def unit(j):
                    if filler:
                        stage, jj = filler[j]
                        split_lo(UNITS[stage] + jj + 1)

                def state_steps(h, t):
                    key = (name, "ds", h, t)
                    dec = hdec[:, h % 2, :]
                    wait_full(dve, key)
                    n = min(cpt, nch - 1 - t * cpt)
                    for c in range(n):
                        i = t * cpt + c
                        src = bank(key)[:, c * w_:(c + 1) * w_]
                        to = states[:, ((i + 1) % slots) * w_:((i + 1) % slots + 1) * w_]
                        if t == 2 and c == n - 1 and nch > slots:
                            seen.next("inter_done")
                        if i == 0:
                            ins = dve.tensor_copy(to, src)
                        else:
                            ins = dve.scalar_tensor_tensor(to, states[:, (i % slots) * w_:(i % slots + 1) * w_],
                                                           dec[:, i:i + 1], src, ALU.mult, ALU.add)
                        if c == n - 1:
                            free(ins, key)
                            wait_drained(dve, key)
                        else:
                            steps.step(ins)
                            steps.wait()

                def normed(h):
                    seen.next("rstd_ready")
                    for d in range(dv):
                        o = out_tile(h, d)
                        steps.step(dve.tensor_tensor(o, o, rstd[:, :], ALU.mult))
                        steps.wait()
                        give(dve.scalar_tensor_tensor(o, o, gain_at(h, d), gate_at(h, d), ALU.mult, ALU.mult), "y_ready")

                def outputs(h):
                    for d in range(dv):
                        give(rest(dv * h + d, out_tile(h, d)), "tile_ready")

                prepare(0)
                if after_first:
                    after_first()
                for h in range(HEADS):
                    key = (name, "scores", h)
                    wait_full(dve, key)
                    free(dve.copy_predicated(sum_x[:, :].rearrange("p (t s) -> p t s", t=TT),
                                             mask.bitcast(U32).unsqueeze(1).broadcast_to([P, TT, P]),
                                             bank(key)[:, :].rearrange("p (t s) -> p t s", t=TT)), key)
                    unit(2 * h)
                    taps(2)
                    if h:
                        mean_square((name, "ssq", h - 1), w_)
                    taps(3)
                    state_steps(h, 0)
                    if h and filler:
                        normed(h - 1)
                    state_steps(h, 1)
                    if h and filler:
                        outputs(h - 1)
                    if not filler:
                        state_steps(h, 2)
                        state_steps(h, 3)
                        if h + 1 < HEADS:
                            prepare(h + 1)
                        if h:
                            normed(h - 1)
                            outputs(h - 1)
                        continue
                    if h + 1 < HEADS:
                        prepare(h + 1)
                    taps(1)
                    state_steps(h, 2)
                    state_steps(h, 3)
                    unit(2 * h + 1)
                    taps(4)
                taps(99)
                mean_square((name, "ssq", HEADS - 1), w_)
                normed(HEADS - 1)
                outputs(HEADS - 1)

            def queries_ahead(split, drain_unit, step, steps):
                for j in range(4):
                    split(j)
                    if j >= 2:
                        step(j - 2)
                    drain_unit(j)
                for s in range(2, steps):
                    step(s)

            def cross_attention(l):
                name = f"xa{l}"

                def step(h):
                    if 1 <= h <= HEADS:
                        g = h - 1
                        wait_drained(dve, (name, "s", g, 1))
                        wait_drained(dve, (name, "s", g, 0))
                        steps.step(dve.reciprocal(rinv[:, g % 2, :], rsum[:, g % 2, :]))
                        steps.wait()
                        for t in range(TT):
                            p_ = pr[:, g % 2, t, :]
                            last = dve.tensor_scalar(p_, p_, rinv[:, g % 2, t:t + 1], None, ALU.mult)
                        give(last, "p_ready")
                    if h < HEADS:
                        for g in range(2):
                            key = (name, "s", h, g)
                            wait_full(dve, key)
                            m = rmax[:, h % 2, 2 * g:2 * g + 2]
                            last = dve.reduce_max(m, bank(key)[:, :].rearrange("p (t n) -> p t n", t=2), AX.X)
                        steps.step(last)
                        steps.wait()
                        m = rmax[:, h % 2, :]
                        give(dve.tensor_scalar(m, m, -1.0, None, ALU.mult), "rowmax_ready")
                    if h >= 2:
                        for d in range(2):
                            key = (name, "o", h - 2, d)
                            wait_full(dve, key)
                            free(rest(2 * (h - 2) + d, bank(key)[:, :]), key)
                    if 1 <= h <= HEADS:
                        key = (name, "pT", h - 1, 1)
                        wait_full(dve, key)
                        free(dve.tensor_copy(pT[:, (h - 1) % 2, 1, :], bank(key)[:, :]), key)
                return step

            dve.wait_ge(prm_loaded, 16)
            lbp = prm[:, COL["lb"]:COL["lb"] + 12].rearrange("p (r h) -> p r h", r=3)
            steps.step(dve.tensor_tensor(lbm[:, :], lbp[:, 0, :], lbp[:, 1, :], ALU.max))
            steps.wait()
            steps.step(dve.tensor_tensor(lbm[:, :], lbm[:, :], lbp[:, 2, :], ALU.max))
            steps.wait()
            give(dve.tensor_tensor(lbs[:, :, :], lbp, lbm[:, :].unsqueeze(1).broadcast_to([P, 3, 4]), ALU.subtract), "lbd_ready")
            for k in range(2):
                give(rest(k, xs[:, k, :]), "tile_ready")
            split_lo(0)
            for k in range(2, KT):
                give(rest(k, xs[:, k, :]), "tile_ready")
            seen.next("lbe_ready")
            steps.step(dve.tensor_tensor(lbm[:, :], lbs[:, 0, :], lbs[:, 1, :], ALU.add))
            steps.wait()
            steps.step(dve.tensor_tensor(lbm[:, :], lbm[:, :], lbs[:, 2, :], ALU.add))
            steps.wait()
            steps.step(dve.reciprocal(lbm[:, :], lbm[:, :]))
            steps.wait()
            steps.step(dve.tensor_tensor(lb0[:, :], lbs[:, 0, :], lbm[:, :], ALU.mult))
            steps.wait()
            steps.step(dve.tensor_scalar(lb1[:, :], lb0[:, :], -1.0, 1.0, ALU.mult, ALU.add))
            split_lo(UNITS["ag0"] + 1)
            sga = hs[:, :].rearrange("p (m t) -> p m t", m=2)

            def conv_input(stage, gates, src):
                for m in range(2):
                    key = (stage, 0, m)
                    wait_full(dve, key)
                    wait_drained(dve, (gates, 0, m))
                    free(dve.tensor_tensor(cu[:, m, TAPS - 1:], src[:, m, :], bank(key)[:, :], ALU.mult), key)
                for m in range(2):
                    wait_drained(dve, (stage, 0, m))

            dve.wait_ge(ones_ready, 3)
            split_lo(UNITS["a0"] + 1)
            conv_input("a0", "ag0", sga)
            conv["it"] = conv_taps(0)
            split_lo(UNITS["ag1"] + 1)
            taps(10)
            for j in range(2):
                split_lo(UNITS["f"] + j + 1)
                taps(9)
                for m in range(2):
                    h = 2 * j + m
                    wait_drained(dve, ("f", j, m))
                    dve.tensor_scalar(hk[:, h, :], hk[:, h, :], lb1[:, h:h + 1], None, ALU.mult)
                    give(dve.tensor_scalar(hb[:, h, :], hb[:, h, :], lb1[:, h:h + 1], lb0[:, h:h + 1], ALU.mult, ALU.add), "f_ready")
            for j in range(2):
                split_lo(UNITS["g"] + j + 1)
                taps(9)
                for m in range(2):
                    key, h = ("g", j, m), 2 * j + m
                    seen.next("gate_ready")
                    wait_full(dve, key)
                    free(dve.tensor_tensor(hg[:, h, :], hg[:, h, :], bank(key)[:, :], ALU.mult), key)
            split_lo(UNITS["a1"] + 1)
            variance("memn", D, MEM)
            taps(99)
            own("conv_ready")
            conv_input("a1", "ag1", cacc[:, 2:4, :])
            conv["it"] = conv_taps(1)
            split_lo(UNITS["q"] + 1)
            seen.next("rstd_ready")
            wait_drained(dve, ("memn", "mean"))
            steps.step(dve.tensor_tensor(mk[:, :, :], mk[:, :, :], mean[:, 0:MEM].unsqueeze(1).broadcast_to([P, KT, MEM]), ALU.subtract))
            steps.wait()
            give(dve.tensor_tensor(mk[:, :, :], mk[:, :, :], rstd[:, 0:MEM].unsqueeze(1).broadcast_to([P, KT, MEM]), ALU.mult), "memz_ready")
            split_lo(UNITS["q"] + 2)
            taps(8)
            seen.next("memn_ready")
            give(dve.tensor_tensor(meml[:, :, :], mk[:, :, :], memh[:, :, :].bitcast(F32), ALU.subtract), "mem_ready")
            split_lo(UNITS["v"] + 1)
            dve.memset(sum_x[:, :], 0.0)
            dve.wait_ge(scan32_loaded, 16)
            for h in range(HEADS):
                seen.next("logf_ready")
                give(dve.tensor_tensor_scan(hb[:, h, :], sum_q[:, :], hb[:, h, :], 0.0, ALU.mult, ALU.add), "b_ready")
            taps(4)
            split_lo(UNITS["v"] + 2)
            for j in range(2):
                wait_drained(dve, ("q", j, 1))
            dve.wait_ge(hmask_loaded, 16)

            def clear_kpad():
                taps(8)
                wait_full(dve, ("v", 1, 1))
                give(dve.memset(kend_hg, 0.0), "kpad_ready")

            linear_attention("hg", 32, hq, hk, hb, heb, henb, hmask[:, :], hs, 1, lambda h, d: hq[:, h, :],
                             lambda h, d: hg[:, h, :], lambda h, d: col("hg_g", h), HG_FILLER, clear_kpad)
            own("conv_ready")
            for k in range(4):
                add_to_sums(k, True, lambda k: cacc[:, k, :], 4)
            normalise("cvn", 512, lambda k: cacc[:, k, :], 4, lambda k: give(rest(4 + k, cacc[:, k, :]), "tile_ready"), UNITS["mixo"])
            residual(pair_keys("mixo"), UNITS["mixo"], 4, True, ALPHA, first=1)
            for l in range(2):
                stage = FILLER[f"mixn{l}"]
                normalise(f"mixn{l}", D, xs_at, KT, rest_of_xs, UNITS[stage], stage)
                queries_ahead(lambda j: j and split_lo(UNITS[f"xq{l}"] + j + 1), lambda j: None, cross_attention(l), HEADS + 2)
                residual(pair_keys(f"xo{l}"), UNITS[f"xo{l}"], 4, True, ALPHA)
                stage = FILLER.get(f"xan{l}")
                normalise(f"xan{l}", D, xs_at, KT, rest_of_xs, UNITS[stage or f"ffn{l}"], stage)
                chunks(f"ffn{l}", True)
                if l == 0:
                    dve.memset(pa[:, :, 0:PAD], 0.0)
                    steps.step(dve.memset(pb[:, :, 0:PAD], 0.0))
                    dve.wait_ge(invpos_loaded, 16)

                    def pool(k):
                        seen.skip("xn_ready", 1)
                        seen.next("x_hi")
                        if k % 2 == 0:
                            if k:
                                pooled(k // 2 - 1)
                            return
                        g = k // 2
                        width = POOL_W[g]
                        a, b = pa[:, 2 * g:2 * g + 2, :], pb[:, :, :]
                        shift = 1
                        while shift < width:
                            steps.wait()
                            steps.step(dve.tensor_tensor(b[:, :, PAD:], a[:, :, PAD:], a[:, :, PAD - shift:PAD + T - shift], ALU.add))
                            a, b = b, a
                            shift *= 2
                        steps.wait()
                        steps.step(dve.tensor_tensor(ptmp[:, :, 0:width], a[:, :, PAD:PAD + width],
                                                     invpos[:, 0:width].unsqueeze(1).broadcast_to([P, 2, width]), ALU.mult))
                        steps.step(dve.scalar_tensor_tensor(pp[:, 2 * g:2 * g + 2, :], a[:, :, PAD:], 1.0 / width,
                                                            xs[:, 2 * g:2 * g + 2, :], ALU.mult, ALU.subtract))
                        steps.wait()
                        for k in (2 * g, 2 * g + 1):
                            give(dve.tensor_tensor(pp[:, k, 0:width], ptmp[:, k % 2, 0:width], xs[:, k, 0:width], ALU.subtract), "pool_ready")

                    def pooled(g):
                        for k in (2 * g, 2 * g + 1):
                            give(rest(k, pp[:, k, :]), "tile_ready")

                    normalise("ffnn0", D, xs_at, KT, pool, UNITS[FILLER["ffnn0"]], FILLER["ffnn0"])
                    pooled(3)
                    keys = [("pool", 0, m) for m in range(KT)]
                    for k in range(KT):
                        seen.next("scaled")
                        wait_full(dve, keys[k])
                        free(dve.scalar_tensor_tensor(xs[:, k, :], bank(keys[k])[:, :], col("pool_s", k), xs[:, k, :],
                                                      ALU.mult, ALU.add), keys[k])
                        sums_behind(k, keys, True)

            def first_rms(k):
                seen.skip("xn_ready", 1)
                give(rest(k, xs[:, k, :], col("mix2_g0", k)), "tile_ready")
                add_to_sums(k, False, xs_at)

            normalise("ffnn1", D, xs_at, KT, first_rms, UNITS["glr"])
            mean_square(("r0", "sq"), D)
            token_rstd("r0")
            seen.next("rstd_ready")
            key = ("glr", 0, 0)
            wait_full(dve, key)
            free(dve.tensor_tensor(glow, bank(key)[:, :], rstd[:, :], ALU.mult), key)
            for j in range(2):
                split_lo(UNITS["gq"] + j + 1)
                for m in range(2):
                    key = ("gq", j, m)
                    wait_full(dve, key)
                    free(dve.scalar_tensor_tensor(gq[:, 2 * j + m, :], bank(key)[:, :], 128.0 ** -0.5, rstd[:, :], ALU.mult, ALU.mult), key)
            for h in range(HEADS):
                key = ("gkz", h)
                wait_full(dve, key)
                free(dve.tensor_scalar(gb[:, h, :], bank(key)[:, :], col("b_gk", h), None, ALU.add), key)
            dve.wait_ge(scan64_loaded, 16)
            for h in range(HEADS):
                seen.next("lsig_ready")
                give(dve.scalar_tensor_tensor(gb[:, h, :], gb[:, h, :], 0.0, sq[:, h % 2, :], ALU.min, ALU.subtract), "z_ready")
                own("z_ready")
                give(dve.tensor_tensor_scan(gb[:, h, :], scan64[:, :], gb[:, h, :], 0.0, ALU.mult, ALU.add), "b_ready")
            for j in range(2):
                split_lo(UNITS["gk"] + j + 1)
                for m in range(2):
                    key = ("gk", j, m)
                    wait_full(dve, key)
                    free(dve.tensor_tensor(gk[:, 2 * j + m, :], bank(key)[:, :], rstd[:, :], ALU.mult), key)
            for j in range(4):
                split_lo(UNITS["gg"] + j + 1)
                for m in range(2):
                    key = ("gg", j, m)
                    wait_full(dve, key)
                    free(dve.tensor_tensor(gg[:, 2 * j + m, :], bank(key)[:, :], rstd[:, :], ALU.mult), key)
            dve.memset(sum_x[:, :], 0.0)
            dve.wait_ge(gmask_loaded, 16)
            give(dve.memset(kend_gla, 0.0), "kpad_ready")
            for j in range(4):
                split_lo(UNITS["gv"] + j + 1)
            seen.next("gate_ready")
            linear_attention("gla", 64, gq, gk, gb, geb, genb, gmask[:, :], gs, 2, lambda h, d: mh[:, h % 2, d, :],
                             lambda h, d: gg[:, 2 * h + d, :], lambda h, d: col("onorm", d), None)
            residual(pair_keys("go"), UNITS["go"], 4, False)
            late_rest("mlp2", 0)
            mean_square(("r1", "sq"), D)
            key = ("vec", 0)
            wait_full(dve, key)
            free(dve.tensor_copy(vt[0:16, 0:384], bank(key)[0:16, 0:384]), key)
            seen.next("rstd_ready")
            chunks("mlp0", False)
            for k in range(KT):
                give(rest(k, xs[:, k, :], col("kvn", k), yh, yl), "tile_ready")
            mean_square(("r2", "sq"), D)
            token_rstd("r2")
            for k in range(KT):
                if k == 2:
                    split_lo(UNITS["sk"] + 1)
                give(rest(k, xs[:, k, :], col("mix2_g1", k)), "tile_ready")
            seen.next("rstd_ready")
            for m in range(2):
                key = ("sk", 0, m)
                wait_full(dve, key)
                free(dve.tensor_tensor(kk[:, m, :], bank(key)[:, :], rstd[:, :], ALU.mult), key)
            split_lo(UNITS["sv"] + 1)
            qv = sf[:, :].rearrange("p (k t) -> p k t", k=KT)
            wait_full(dve, ("bias", 7))

            def scaled_queries(j):
                for m in range(2):
                    key = ("sq", j, m)
                    wait_full(dve, key)
                    free(dve.scalar_tensor_tensor(qv[:, 2 * j + m, :], bank(key)[:, :], 0.125, rstd[:, :], ALU.mult, ALU.mult), key)
            dve.wait_ge(sinks_loaded, 16)
            for m in range(8):
                wait_drained(dve, ("bias", m))

            def swa(it):
                if 1 <= it <= SWA_ITEMS:
                    g = it - 1
                    for j in range(2):
                        seen.next("e_ready")
                        d_ = rinv[:, g % 2, 2 * j:2 * j + 2]
                        steps.step(dve.tensor_tensor(d_, rsum[:, g % 2, 2 * j:2 * j + 2], rsnk[:, g % 2, 2 * j:2 * j + 2], ALU.add))
                        steps.wait()
                        steps.step(dve.reciprocal(d_, d_))
                        steps.wait()
                        for n in range(2):
                            lo = P if g % 2 == 0 and n == 0 else 0
                            p_ = mh[:, g % 2, j, n * 256 + lo:(n + 1) * 256]
                            last = dve.tensor_scalar(p_, p_, rinv[:, g % 2, 2 * j + n:2 * j + n + 1], None, ALU.mult)
                        give(last, "p_ready")
                if it < SWA_ITEMS:
                    hp, nn = it // 2, it % 2
                    for j in range(2):
                        key, h = ("swa", "s", it, j), 2 * hp + j
                        s_ = mh[:, it % 2, j, :]
                        m_ = rmax[:, it % 2, 2 * j:2 * j + 2]
                        wait_full(dve, key)
                        if nn == 0:
                            dve.tensor_tensor(s_[:, P:2 * P], bank(key)[:, P:2 * P], bias[:, h, P:2 * P], ALU.add)
                            free(dve.tensor_tensor(s_[:, 2 * P:], bank(key)[:, 2 * P:], bias[:, h, :], ALU.add), key)
                            wait_drained(dve, key)
                            dve.reduce_max(m_[:, 0:1], s_[:, P:2 * P], AX.X)
                            steps.step(dve.reduce_max(m_[:, 1:2], s_[:, 2 * P:], AX.X))
                        else:
                            free(dve.tensor_tensor(s_.rearrange("p (n k) -> p n k", n=2), bank(key)[:, :].rearrange("p (n k) -> p n k", n=2),
                                                   bias[:, h, :].unsqueeze(1).broadcast_to([P, 2, 2 * P]), ALU.add), key)
                            wait_drained(dve, key)
                            steps.step(dve.reduce_max(m_, s_.rearrange("p (n k) -> p n k", n=2), AX.X))
                        steps.wait()
                        give(dve.tensor_scalar(m_, m_, skb[:, h:h + 1], -1.0, ALU.max, ALU.mult), "rowmax_ready")
                if it >= 2 and it % 2:
                    hp = (it - 2) // 2
                    key = ("swa", "o", hp)
                    free(rest(hp, bank(key)[:, :]), key)

            queries_ahead(lambda j: split_lo(UNITS["sq"] + j + 1), scaled_queries, swa, SWA_ITEMS + 2)
            residual(pair_keys("so"), UNITS["so"], 4, False)
            late_rest("mlp2", 1)
            mean_square(("r3", "sq"), D)
            seen.next("rstd_ready")
            chunks("mlp1", False)
            mean_square(("fin", "sq"), D)
            seen.next("rstd_ready")
            for k in range(KT):
                give(dve.scalar_tensor_tensor(xs[:, k, :], xs[:, k, :], col("fin_g", k), rstd[:, :], ALU.mult, ALU.mult), "out_ready")


def units(name, a, k_tiles, cols):
    K, M = a.shape
    a = a.reshape(K // (k_tiles * P), k_tiles, P, M // cols, cols)
    return a.transpose(0, 3, 2, 1, 4).reshape(-1, P, UNIT)


def pack_weights(i):
    def wide(a):
        return units("", a, KT, 256)

    def narrow(a):
        u = np.zeros((1, P, UNIT), np.float32)
        u[0, :, :KT * P] = a.reshape(KT, P, P).transpose(1, 0, 2).reshape(P, KT * P)
        return u

    ab, gla, kv = i["ab_w_in"][0], i["a_w_in_2"][0], i["w_kv_2"]
    hw = HEADS * P
    out = {"ag0": wide(ab[:, 5 * hw:5 * hw + 256]), "a0": wide(ab[:, 4 * hw:4 * hw + 256]),
           "ag1": wide(ab[:, 5 * hw + 256:6 * hw]), "a1": wide(ab[:, 4 * hw + 256:5 * hw]),
           "q": wide(ab[:, 0:hw]), "f": wide(ab[:, hw:2 * hw]), "v": wide(ab[:, 2 * hw:3 * hw]), "g": wide(ab[:, 3 * hw:4 * hw]),
           "mixo": wide(i["ab_w_out"][0]),
           "pool": i["pool_w"][0].reshape(4, 2, P, 256).transpose(2, 0, 1, 3).reshape(1, P, UNIT),
           "gq": wide(gla[:, 0:512]), "gk": wide(gla[:, 512:1024]), "gv": wide(gla[:, 1024:2048]), "gg": wide(gla[:, 2048:3072]),
           "glr": narrow(gla[:, 3088 - P:3088]), "go": wide(i["a_w_out_2"][0]),
           "sk": wide(np.concatenate([kv[:, 0:64], kv[:, 0:64], kv[:, 64:128], kv[:, 64:128]], axis=1)),
           "sv": narrow(kv[:, 128:256]), "sq": wide(i["b_w_q_2"][0]), "so": wide(i["b_w_out_2"][0])}

    def in_chunks(ups, down):
        u = [wide(a) for a in ups]
        d = units("", down, 2, D)
        n = len(d)
        order = [a[0] for a in u]
        for c in range(n):
            if c + 1 < n:
                order += [a[c + 1] for a in u]
            order.append(d[c])
        return np.stack(order)

    for l in range(2):
        for name, w in (("mk", i["xa_wk"]), ("mv", i["xa_wv"])):
            u = wide(w[l])
            if l == 0:
                out[name + "0"] = u
            else:
                out[name + "1a"], out[name + "1b"] = u[:2], u[2:]
        out[f"xq{l}"], out[f"xo{l}"] = wide(i["xa_wq"][l]), wide(i["xa_wo"][l])
        out[f"ffn{l}"] = in_chunks((i["ffn_wg"][l], i["ffn_wu"][l]), i["ffn_wd"][l])
        out[f"mlp{l}"] = in_chunks((i["w_up_2"][l],), i["w_down_2"][l])
    return np.concatenate([out[name] for name, _ in STAGES])


def pack_params(i):
    v = {"mem_g": i["mem_ln_g"], "mem_b": i["mem_ln_b"], "lb": i["lb_param"], "hg_g": i["hg_norm_g"][0],
         "cv_b": i["cv_b"][0], "cv_g": i["cv_ln_g"][0], "cv_lb": i["cv_ln_b"][0], "pool_s": i["pool_scale"][0],
         "cv_w": i["cv_w"][0][:, 0, :].reshape(TAPS, 4, P).transpose(1, 0, 2),
         "b_gk": i["a_b_gk_2"][0], "onorm": i["a_onorm_2"][0], "kvn": i["kv_norm_2"], "fin_g": i["ln_final_2"]}
    for l in range(2):
        for ours, theirs in (("mix", "ln_mix"), ("xa", "ln_xa"), ("ffn", "ln_ffn")):
            v[f"{ours}_g{l}"], v[f"{ours}_b{l}"] = i[f"{theirs}_g"][l], i[f"{theirs}_b"][l]
        v[f"mix2_g{l}"], v[f"mlp2_g{l}"] = i["ln_mix_2"][l], i["ln_mlp_2"][l]
    return np.concatenate([v[name].reshape(n, P) for name, n in PARAMS]).T


def kernel(**inputs):
    import concourse.bacc as bacc
    from concourse.bass_utils import run_bass_kernel_spmd

    i = {k: np.asarray(v) for k, v in inputs.items()}
    arrays = {
        "x_in": i["x"][0].reshape(T, KT, P).transpose(2, 1, 0),
        "mem_in": i["mem"][0].reshape(MEM, KT, P).transpose(2, 1, 0),
        "params_in": pack_params(i),
        "consts_in": constants(),
        "table_in": i["rel_table_2"],
        "w_gk2_in": i["a_w_gk2_2"][0],
        "sinks_in": i["b_sinks_2"][0],
        "weights_in": pack_weights(i),
    }
    nc = bacc.Bacc("TRN2", target_bir_lowering=False, num_devices=1)
    args = []
    for name, a in arrays.items():
        a = arrays[name] = np.ascontiguousarray(a)
        args.append(nc.dram_tensor(name, a.shape, mybir.dt.from_np(a.dtype), kind="ExternalInput").ap())
    args.append(nc.dram_tensor("y_out", (P, KT, T), F32, kind="ExternalOutput").ap())
    build(nc, *args)
    r = run_bass_kernel_spmd(nc, [arrays], core_ids=[0])
    y = r.results[0]["y_out"]
    return y.transpose(2, 1, 0).reshape(1, T, D)
```
